# Optimizing a Trainium2 kernel written in Bass

```python
import math
import jax, jax.numpy as jnp
from jax import lax
import numpy as np

D_MODEL = 1024
BATCH = 1
SEQ = 512
DEPTH = 1
DEC_BATCH = 8
DEC_SEQ = 8
PAST_LEN = 2048
PAGE_SIZE = 128

D_MIX = D_MODEL
D_ATT = D_MIX // 2
D_CONV = D_MIX - D_ATT
HEAD_DIM = 64
N_HEADS = D_ATT // HEAD_DIM
CONV_WIDTH = 3
DILATED_PAIRS = ((128, 1), (512, 4), (2048, 16))
MAX_WINDOW = max(w for w, _ in DILATED_PAIRS)
Q_BLOCK = 128
LN_EPS = 1e-5
DEEPNORM_ALPHA = (2.0 * DEPTH) ** 0.25
DEEPNORM_BETA = (8.0 * DEPTH) ** -0.25
SPLIT_SIZES = (D_ATT, D_ATT, D_ATT, D_ATT, D_CONV, D_CONV, D_CONV, D_CONV)
D_IN = sum(SPLIT_SIZES)

kernel_name = "hymba_dilated_swa_shortconv_step"

def _dilated_branch(q, k_all, v_all, window, dilation, offset):
    b, t, h, dh = q.shape
    n_keys = window // dilation + 1
    qb = math.gcd(t, Q_BLOCK)
    n_blk = t // qb
    dist = dilation * jnp.arange(n_keys, dtype=jnp.int32)
    scale = dh ** -0.5

    def block(start):
        q_blk = lax.dynamic_slice_in_dim(q, start, qb, axis=1)
        q_idx = offset + start + jnp.arange(qb, dtype=jnp.int32)
        idx = q_idx[:, None] - dist[None, :]
        valid = idx >= 0
        idx = jnp.maximum(idx, 0)
        k_g = jnp.take(k_all, idx, axis=1)
        v_g = jnp.take(v_all, idx, axis=1)
        s = jnp.einsum('bqhd,bqjhd->bhqj', q_blk, k_g).astype(jnp.float32) * scale
        s = jnp.where(valid[None, None], s, -jnp.inf)
        lse = jax.nn.logsumexp(s, axis=-1)
        p = jnp.exp(s - lse[..., None]).astype(v_all.dtype)
        o = jnp.einsum('bhqj,bqjhd->bqhd', p, v_g)
        return o, lse

    o, lse = lax.map(block, jnp.arange(n_blk, dtype=jnp.int32) * qb)
    o = jnp.moveaxis(o, 0, 1).reshape(b, t, h, dh)
    lse = jnp.transpose(lse, (1, 0, 3, 2)).reshape(b, t, h)
    return o, lse

def _dilated_attention(q, k_all, v_all, offset):
    outs, lses = [], []
    for window, dilation in DILATED_PAIRS:
        o, lse = _dilated_branch(q, k_all, v_all, window, dilation, offset)
        outs.append(o)
        lses.append(lse)
    wts = jax.nn.softmax(jnp.stack(lses, axis=0), axis=0)
    return jnp.einsum('rbth,rbthd->bthd', wts.astype(q.dtype), jnp.stack(outs, axis=0))

def _layer_norm(x, g, b):
    xf = x.astype(jnp.float32)
    mu = jnp.mean(xf, axis=-1, keepdims=True)
    var = jnp.mean(jnp.square(xf - mu), axis=-1, keepdims=True)
    y = (xf - mu) * lax.rsqrt(var + LN_EPS) * g.astype(jnp.float32) + b.astype(jnp.float32)
    return y.astype(x.dtype)

def _hybrid_layer(x, k_past, v_past, conv_past, w_in, conv_w, w_out, ln_g, ln_b):
    bsz, t, _ = x.shape
    proj = jnp.einsum('btd,de->bte', x, w_in)
    q, k, v, g_att, gb, gc, hh, g_conv = jnp.split(
        proj, [int(s) for s in np.cumsum(SPLIT_SIZES)[:-1]], axis=-1)
    q = q.reshape(bsz, t, N_HEADS, HEAD_DIM)
    k = k.reshape(bsz, t, N_HEADS, HEAD_DIM)
    v = v.reshape(bsz, t, N_HEADS, HEAD_DIM)

    if k_past is None:
        k_all, v_all, offset = k, v, 0
    else:
        k_all = jnp.concatenate([k_past, k], axis=1)
        v_all = jnp.concatenate([v_past, v], axis=1)
        offset = k_past.shape[1]
    o_att = _dilated_attention(q, k_all, v_all, offset).reshape(bsz, t, D_ATT)
    att = o_att * jax.nn.silu(g_att)

    u = gc * hh
    u_pad = jnp.concatenate([conv_past.astype(u.dtype), u], axis=1)
    y_conv = conv_w[0] * u_pad[:, 0:t]
    for j in range(1, CONV_WIDTH):
        y_conv = y_conv + conv_w[j] * u_pad[:, j:j + t]
    z = gb * y_conv * jax.nn.silu(g_conv)

    mix = jnp.concatenate([att, z], axis=-1)
    out = jnp.einsum('bte,ed->btd', mix, w_out)
    y = _layer_norm(DEEPNORM_ALPHA * x + out, ln_g, ln_b)

    n_all = k_all.shape[1]
    keep = min(MAX_WINDOW, n_all)
    new_k = k_all[:, n_all - keep:]
    new_v = v_all[:, n_all - keep:]
    new_conv = u_pad[:, t:]
    return y, new_k, new_v, new_conv

def setup_inputs(seed: int = 0) -> dict:
    key = jax.random.key(seed)
    ks = jax.random.split(key, 10)
    win_buf = min(MAX_WINDOW, PAST_LEN)
    x_prompt = jax.random.normal(ks[0], (BATCH, SEQ, D_MODEL), jnp.float32)
    x_sample = jax.random.normal(ks[1], (DEC_BATCH, DEC_SEQ, D_MODEL), jnp.float32)
    cache_k = jax.random.normal(ks[2], (DEC_BATCH, win_buf, N_HEADS, HEAD_DIM), jnp.float32)
    cache_v = jax.random.normal(ks[3], (DEC_BATCH, win_buf, N_HEADS, HEAD_DIM), jnp.float32)
    state_conv = jax.random.normal(ks[4], (DEC_BATCH, CONV_WIDTH - 1, D_CONV), jnp.float32)
    w_in = jax.random.normal(ks[5], (D_MODEL, D_IN), jnp.float32) * D_MODEL ** -0.5
    conv_w = jax.random.normal(ks[6], (CONV_WIDTH, D_CONV), jnp.float32) * CONV_WIDTH ** -0.5
    w_out = jax.random.normal(ks[7], (D_MIX, D_MODEL), jnp.float32) * (D_MIX ** -0.5) * DEEPNORM_BETA
    ln_g = 1.0 + 0.1 * jax.random.normal(ks[8], (D_MODEL,), jnp.float32)
    ln_b = 0.01 * jax.random.normal(ks[9], (D_MODEL,), jnp.float32)
    return {"x_prompt": x_prompt, "x_sample": x_sample, "cache_k": cache_k,
            "cache_v": cache_v, "state_conv": state_conv, "w_in": w_in,
            "conv_w": conv_w, "w_out": w_out, "ln_g": ln_g, "ln_b": ln_b}

def reference(x_prompt, x_sample, cache_k, cache_v, state_conv, w_in, conv_w, w_out, ln_g, ln_b):
    y_prompt = x_prompt
    y_sample = x_sample
    conv0 = jnp.zeros((x_prompt.shape[0], CONV_WIDTH - 1, D_CONV), x_prompt.dtype)
    for _layer in range(DEPTH):
        y_prompt, new_k_prompt, new_v_prompt, new_conv_prompt = _hybrid_layer(
            y_prompt, None, None, conv0, w_in, conv_w, w_out, ln_g, ln_b)
        y_sample, new_k_sample, new_v_sample, new_conv_sample = _hybrid_layer(
            y_sample, cache_k, cache_v, state_conv, w_in, conv_w, w_out, ln_g, ln_b)
    return (y_prompt, y_sample, new_k_prompt, new_v_prompt, new_conv_prompt,
            new_k_sample, new_v_sample, new_conv_sample)


_drawn_inputs = setup_inputs


def setup_inputs(seed=0):
    import zlib

    import numpy as np

    out = dict(_drawn_inputs(seed))
    spreads = {}
    factors = {'ln_b': 5.739}
    for name, (base, spread) in spreads.items():
        noise = np.random.default_rng([zlib.crc32(name.encode()), seed]).standard_normal(out[name].shape)
        drawn = base * np.exp(spread * noise) if base else spread * noise
        out[name] = __import__('jax').numpy.asarray(drawn.astype(out[name].dtype))
    for name, factor in factors.items():
        out[name] = (out[name] * factor).astype(out[name].dtype)
    return out
```

```python
from contextlib import ExitStack

import numpy as np

import concourse.bass as bass
from concourse import mybir

P = 128
D_MODEL = 1024
SEQ = 512
DEC_BATCH = 8
DEC_SEQ = 8
PAST_LEN = 2048
N_HEADS = 8
HEAD_DIM = 64
D_ATT = N_HEADS * HEAD_DIM
CONV_WIDTH = 3
PAIRS = ((128, 1), (512, 4), (2048, 16))
LN_EPS = 1e-5
ALPHA = 2.0 ** 0.25
SCALE = HEAD_DIM ** -0.5

NS = DEC_BATCH * DEC_SEQ
NT = SEQ + NS
HALF = NT // 2
HP_LEFT = SEQ - HALF
KT = D_MODEL // P
NHP = D_ATT // P
NPAIR = DEC_BATCH // 2
QKV_TILES = 3 * NHP
ROUND_TILES = 5
W_TILES = QKV_TILES + NPAIR * ROUND_TILES
USED_TILES = 10
USED = USED_TILES * P
REST = PAST_LEN - USED
REST_ROWS = DEC_BATCH * REST * D_ATT // (256 * 1024)
S_COLS = USED + NS
V_PIECES = 10
V_SLOTS = 5
QT = SEQ // P
UNITS = 2 * QT
UNIT_ORDER = [(e, t) for t in reversed(range(QT)) for e in range(2)]
CHUNKS = ((0, 512), (512, 512), (1024, 256))
PAD_COLS = 2 + SEQ + DEC_BATCH * (2 + DEC_SEQ)
NEG = -1e30
BIG = 3e38

F32 = mybir.dt.float32
F32R = mybir.dt.float32r
ALU = mybir.AluOpType
ACT = mybir.ActivationFunctionType
AX_X = mybir.AxisListType.X


def on_all_partitions(row):
    return bass.AP(tensor=row.tensor, offset=row.offset, ap=[[0, P], [1, row.shape[-1]]])


def layer_step(nc, d):
    with ExitStack() as ctx:
        def sb(name, shape, dt=F32, stack=ctx):
            return stack.enter_context(nc.sbuf_tensor(name, shape, dt))

        def bank(name):
            return ctx.enter_context(nc.psum_tensor(name, [P, 512], F32))

        def sem(name):
            return ctx.enter_context(nc.semaphore(name))

        x_hi = sb("x_hi", [P, KT * NT], F32R)
        x_lo = sb("x_lo", [P, KT * NT], F32R)
        w_raw = sb("w_raw", [P, 2 * 1024])
        w_hi = sb("w_hi", [P, 2 * 1024], F32R)
        w_lo = sb("w_lo", [P, 2 * 1024], F32R)
        mix = sb("mix", [P, 2 * NHP * NT])
        gcs = sb("gcs", [P, NT])
        zb = sb("zb", [P, NT])
        rg = sb("rg", [P, NT])
        u_pad = sb("u_pad", [P, PAD_COLS])
        y_pad = sb("y_pad", [P, PAD_COLS])
        att_s = sb("att_s", [P, NHP * NS])
        new_conv = sb("new_conv", [P, NHP * 2 * (1 + DEC_BATCH)])
        state = sb("state", [P, NHP * 2 * DEC_BATCH])
        conv_w = sb("conv_w", [P, NHP * CONV_WIDTH])
        cw = sb("cw", [P, CONV_WIDTH])
        ident = sb("ident", [P, P])
        stat = sb("stat", [P, 48])
        early = ctx.enter_context(ExitStack())
        k_buf = sb("k_buf", [P, 2 * 2560], stack=early)
        qk = sb("qk", [P, 2 * NHP * NT], stack=early)
        v_rows = sb("v_rows", [P, QT * D_ATT], stack=early)
        q_st = sb("q_st", [P, SEQ], stack=early)
        k_st = sb("k_st", [P, SEQ], stack=early)
        v_st = sb("v_st", [P, SEQ], stack=early)
        p_pr = sb("p_pr", [P, 2 * 512], stack=early)
        pt_pr = sb("pt_pr", [P, 2 * 512], stack=early)
        p_s = sb("p_s", [P, S_COLS], stack=early)
        v_new = sb("v_new", [NS, D_ATT], stack=early)
        v_buf = sb("v_buf", [P, V_SLOTS * 1024], stack=early)
        pt_s = sb("pt_s", [P, (USED_TILES + 1) * P], stack=early)
        o_s = sb("o_s", [P, D_ATT], stack=early)
        o_pr = sb("o_pr", [P, SEQ], stack=early)
        mask_s = sb("mask_s", [P, S_COLS], stack=early)
        mask_new = sb("mask_new", [P, NPAIR * NS], stack=early)
        mask_pr = sb("mask_pr", [P, SEQ], stack=early)
        q_bd = sb("q_bd", [P, NHP * P], stack=early)
        early.close()
        wo = sb("wo", [P, KT * 2 * 1024], F32R)
        ln_g = sb("ln_g", [P, D_MODEL])
        ln_b = sb("ln_b", [P, D_MODEL])
        x_res = sb("x_res", [P, 2 * D_MODEL])
        y_t = sb("y_t", [P, 2 * D_MODEL])

        pj_a, pj_b = bank("pj_a"), bank("pj_b")
        sc = [bank(f"sc{c}") for c in range(3)]
        px, pt, po = bank("px"), bank("pt"), bank("po")

        x_in = [sem(f"x_in{n}") for n in range(4)]
        small_in, ln_in = sem("small_in"), sem("ln_in")
        res_in = [sem("res_in0"), sem("res_in1")]
        w_in = [sem("w_in0"), sem("w_in1")]
        k_in = [sem("k_in0"), sem("k_in1")]
        v_in = [sem(f"v_in{n}") for n in range(V_SLOTS)]
        kv_out, copied, conv_out = sem("kv_out"), sem("copied"), sem("conv_out")
        y_out = [sem("y_out0"), sem("y_out1")]
        x_hi_done, x_lo_done = sem("x_hi_done"), sem("x_lo_done")
        w_hi_done, w_lo_done = sem("w_hi_done"), sem("w_lo_done")
        pj_a_done, pj_b_done = sem("pj_a_done"), sem("pj_b_done")
        qkv_a_read, qkv_b_read = sem("qkv_a_read"), sem("qkv_b_read")
        c_read = [sem("c_read_a"), sem("c_read_b")]
        vt_done, vt_read, vn_read = sem("vt_done"), sem("vt_read"), sem("vn_read")
        staged, zeroed, qbd_done, masked_new, padded = (
            sem("staged"), sem("zeroed"), sem("qbd_done"), sem("masked_new"), sem("padded"))
        u_done, y_done, z_done, new_conv_done = sem("u_done"), sem("y_done"), sem("z_done"), sem("new_conv_done")
        y_step, may_mask = sem("y_step"), sem("may_mask")
        k_used, v_used = sem("k_used"), sem("v_used")
        pr_scores, pr_masked, pr_exp, pr_inv, pr_norm = (
            sem("pr_scores"), sem("pr_masked"), sem("pr_exp"), sem("pr_inv"), sem("pr_norm"))
        pr_turned, pr_moved, pr_pv, pr_out = sem("pr_turned"), sem("pr_moved"), sem("pr_pv"), sem("pr_out")
        s_masked, s_max, s_exp, s_inv, s_norm = (
            sem("s_masked"), sem("s_max"), sem("s_exp"), sem("s_inv"), sem("s_norm"))
        s_turned, s_moved, s_pv, s_out = sem("s_turned"), sem("s_moved"), sem("s_pv"), sem("s_out")
        so_turned, so_moved = sem("so_turned"), sem("so_moved")
        g_exp, g_step, mixed = sem("g_exp"), sem("g_step"), sem("mixed")
        m_hi_done, m_lo_done, wo_hi_done, wo_lo_done = (
            sem("m_hi_done"), sem("m_lo_done"), sem("wo_hi_done"), sem("wo_lo_done"))
        o_done, r_done, ln_step, ln_sqrt, ln_scaled, ln_done = (
            sem("o_done"), sem("r_done"), sem("ln_step"), sem("ln_sqrt"), sem("ln_scaled"), sem("ln_done"))

        x_raw = k_buf[:, 0:KT * NT]
        v_stage = [gcs, zb]
        u_s = u_pad[:, 2 + SEQ:].rearrange("p (b t) -> p b t", t=2 + DEC_SEQ)
        y_s = y_pad[:, 2 + SEQ:].rearrange("p (b t) -> p b t", t=2 + DEC_SEQ)
        negmax_pr, sum_pr, inv_pr = stat[:, 0:2], stat[:, 2:4], stat[:, 4:6]
        negmax3, negmax_s, sum_s, inv_s = stat[:, 6:9], stat[:, 9:10], stat[:, 10:11], stat[:, 11:12]
        bn, mv, rstd = stat[:, 12:24], stat[:, 24:26], stat[:, 26:27]
        std = stat[:, 27:28]

        def qbd_copy_ap(e):
            a = q_bd[e * 64:e * 64 + 64, e * 8:e * 8 + 8]
            return bass.AP(tensor=a.tensor, offset=a.offset, ap=[[NHP * P, 64], [P + 16, NHP], [64, 2], [1, 8]])

        def diagonal_ap(e):
            a = pt[e * 64:e * 64 + 64, e * 8:e * 8 + 8]
            return bass.AP(tensor=a.tensor, offset=a.offset, ap=[[512, 64], [P + 16, NHP], [64, 2], [1, 8]])

        block = ctx.enter_context(nc.Block())

        @block.sync
        def _(sp):
            def load_w(tile, slot, split_before):
                if split_before is not None:
                    sp.wait_ge(w_lo_done, split_before)
                sp.dma_start(w_raw[:, slot * 1024:(slot + 1) * 1024],
                             d["w_tiles"][bass.ds(tile * P, P), :]).then_inc(w_in[slot], 16)

            def copy_rest(row):
                for name in ("k_rest", "v_rest"):
                    sp.dma_start(d[name + "_out"][bass.ds(row * 256, 256), :],
                                 d[name][bass.ds(row * 256, 256), :]).then_inc(copied, 16)

            for n in range(4):
                c = slice(n * 2 * NT, (n + 1) * 2 * NT)
                sp.dma_start(x_raw[:, c], d["xT"][:, c]).then_inc(x_in[n], 16)
                if n < 2:
                    load_w(n, n, None)
            sp.dma_start(ident[:, :], d["ident"]).then_inc(small_in, 16)
            sp.dma_start(mask_pr[:, :], d["mask_pr"]).then_inc(small_in, 16)
            sp.dma_start(mask_new[:, :], d["mask_new"]).then_inc(small_in, 16)
            sp.dma_start(mask_s[:, 0:USED], d["mask_s"]).then_inc(small_in, 16)
            sp.dma_start(state[:, :], d["state"]).then_inc(small_in, 16)
            sp.dma_start(conv_w[:, :], d["conv_w"]).then_inc(small_in, 16)

            with sp.Fori(0, QKV_TILES // 2 - 1) as m:
                for j in range(2):
                    load_w(2 * m + 2 + j, j, 2 * m + 1 + j)
                copy_rest(m)
            sp.wait_ge(qkv_a_read, 2 * NHP)
            sp.wait_ge(qkv_b_read, 2 * NHP)
            sp.dma_start(d["kT_new"], qk[:, NHP * NT:]).then_inc(kv_out, 16)
            sp.wait_ge(vt_read, NHP)
            sp.dma_start(d["v_prompt"].rearrange("(t p) n -> p t n", p=P),
                         v_rows[:, :].rearrange("p (t n) -> p t n", t=QT)).then_inc(kv_out, 16)
            sp.wait_ge(vn_read, NHP)
            sp.dma_start(d["v_sample"], v_new[:, :]).then_inc(kv_out, 16)

            with sp.Fori(0, NPAIR) as i:
                t0 = QKV_TILES + ROUND_TILES * i

                def load_k(hp):
                    sp.wait_ge(k_used, 1 + 4 * i + max(0, hp - 1))
                    sp.dma_start(k_buf[:, hp % 2 * 2560:(hp % 2 + 1) * 2560],
                                 d["k_used"][bass.ds((4 * i + hp) * P, P), :]).then_inc(k_in[hp % 2], 16)

                def load_v(n):
                    sp.wait_ge(v_used, 1 + V_PIECES * i + max(0, n - V_SLOTS + 1))
                    slot = n % V_SLOTS
                    sp.dma_start(v_buf[:, slot * 1024:(slot + 1) * 1024],
                                 d["v_used"][bass.ds((V_PIECES * i + n) * P, P), :]).then_inc(v_in[slot], 16)

                def copy_k(hp):
                    sp.dma_start(d["k_used_out"][bass.ds((4 * i + hp) * P, P), :],
                                 d["k_used"][bass.ds((4 * i + hp) * P, P), :]).then_inc(copied, 16)

                def copy_v(s):
                    sp.dma_start(d["v_used_out"][bass.ds((V_PIECES * i + 2 * s) * P, 2 * P), :],
                                 d["v_used"][bass.ds((V_PIECES * i + 2 * s) * P, 2 * P), :]).then_inc(copied, 16)

                load_w(t0, 0, t0)
                load_w(t0 + 1, 1, t0)
                load_k(0)
                load_k(1)
                copy_k(0)
                for n in range(V_SLOTS):
                    load_v(n)
                copy_k(1)
                load_w(t0 + 2, 0, t0 + 1)
                copy_k(2)
                copy_k(3)
                load_w(t0 + 3, 1, t0 + 2)
                load_k(2)
                copy_v(0)
                load_k(3)
                copy_v(1)
                copy_v(2)
                load_w(t0 + 4, 0, t0 + 3)
                copy_v(3)
                load_v(5)
                load_v(6)
                copy_v(4)
                load_v(7)
                load_v(8)
                copy_rest(QKV_TILES // 2 - 1 + i)
                load_v(9)
            for k in range(KT):
                load_w(W_TILES + k, k % 2, W_TILES + max(0, k - 1))
            for row in range(QKV_TILES // 2 - 1 + NPAIR, REST_ROWS):
                copy_rest(row)
            sp.wait_ge(s_pv, 1 + NPAIR)
            sp.wait_ge(kv_out, 48)
            sp.dma_start(ln_g[:, :], on_all_partitions(d["ln_g"])).then_inc(ln_in, 16)
            sp.dma_start(ln_b[:, :], on_all_partitions(d["ln_b"])).then_inc(ln_in, 16)
            sp.wait_ge(new_conv_done, 1 + 2 * NPAIR)
            sp.dma_start(d["new_conv"], new_conv[:, :]).then_inc(conv_out, 16)
            for t in range(QT + 1):
                rows = P if t < QT else NS
                if t >= 2:
                    sp.wait_ge(r_done, 2 * (t - 1))
                sp.dma_start(x_res[0:rows, t % 2 * 1024:(t % 2 + 1) * 1024],
                             d["x_rows"][t * P:t * P + rows, :]).then_inc(res_in[t % 2], 16)
                if t >= 1:
                    sp.wait_ge(ln_done, t)
                    sp.dma_start(d["y"][(t - 1) * P:t * P, :],
                                 y_t[:, (t - 1) % 2 * 1024:((t - 1) % 2 + 1) * 1024]).then_inc(y_out[(t - 1) % 2], 16)
            sp.wait_ge(ln_done, QT + 1)
            sp.dma_start(d["y"][SEQ:NT, :], y_t[0:NS, QT % 2 * 1024:(QT % 2 + 1) * 1024]).then_inc(y_out[QT % 2], 16)
            sp.wait_ge(y_out[0], 16 * 3)
            sp.wait_ge(y_out[1], 16 * 2)
            sp.wait_ge(conv_out, 16)
            sp.wait_ge(copied, 16 * (2 * REST_ROWS + NPAIR * (NHP + V_PIECES // 2)))

        @block.gpsimd
        def _(pool):
            for opened in (new_conv_done,):
                pool.sem_inc(opened, 1)
            pool.memset(q_bd[:, :], 0.0).then_inc(zeroed, 1)
            pool.memset(u_pad[:, 0:2], 0.0).then_inc(zeroed, 1)
            pool.wait_ge(zeroed, 2)
            pool.wait_ge(small_in, 96)
            pool.wait_ge(qkv_a_read, 2 * NHP)
            pool.wait_ge(qkv_b_read, 2 * NHP)
            pool.wait_ge(vt_read, NHP)
            with pool.Fori(0, NPAIR) as i:
                pool.wait_ge(pr_pv, 1 + UNITS * i)
                pool.tensor_copy(q_st[:, :], qk[:, bass.ds(i * NT, SEQ)]).then_inc(staged, 1)
                pool.tensor_copy(k_st[:, :], qk[:, bass.ds((NHP + i) * NT, SEQ)]).then_inc(staged, 1)
                pool.tensor_copy(v_st[:, :].rearrange("p (t n) -> p t n", t=QT),
                                 v_rows[:, :].rearrange("p (t n) -> p t n", t=QT)[:, :, bass.ds(i * P, P)])\
                    .then_inc(staged, 1)
                pool.wait_ge(staged, 3 * i + 3)
                pool.wait_ge(k_used, 1 + 4 * i)
                for e in range(2):
                    src = qk[e * 64:e * 64 + 64, 0:NHP * NT].rearrange("p (h t) -> p h t", t=NT)[
                        :, :, bass.ds(SEQ + 16 * i, 16)].rearrange("p h (b q) -> p h b q", b=2)
                    pool.tensor_copy(qbd_copy_ap(e), src).then_inc(qbd_done, 1)
                    pool.wait_ge(qbd_done, 2 * i + e + 1)
                pool.wait_ge(s_masked, 1 + 3 * i)
                pool.tensor_copy(mask_s[:, USED:], mask_new[:, bass.ds(i * NS, NS)]).then_inc(masked_new, 1)
                pool.wait_ge(y_done, 1 + i)
                pool.wait_ge(new_conv_done, 1 + 2 * i)
                pool.tensor_copy(cw[:, :], conv_w[:, bass.ds(i * CONV_WIDTH, CONV_WIDTH)]).then_inc(padded, 1)
                pool.tensor_copy(u_s[:, :, 0:2],
                                 state[:, bass.ds(i * 2 * DEC_BATCH, 2 * DEC_BATCH)].rearrange("p (b t) -> p b t", t=2))\
                    .then_inc(padded, 1)
                pool.wait_ge(u_done, 1 + 3 * i + 3)
                pool.tensor_copy(new_conv[:, bass.ds(i * 18, 2)], u_pad[:, SEQ:SEQ + 2]).then_inc(new_conv_done, 1)
                pool.tensor_copy(new_conv[:, bass.ds(i * 18 + 2, 16)].rearrange("p (b t) -> p b t", t=2),
                                 u_s[:, :, DEC_SEQ:DEC_SEQ + 2]).then_inc(new_conv_done, 1)

        @block.scalar
        def _(act):
            for opened in (s_out, so_moved):
                act.sem_inc(opened, 1)

            def split_hi(slot, loaded, used_before):
                act.wait_ge(w_in[slot], 16 * loaded)
                if used_before is not None:
                    act.wait_ge(pj_b_done, used_before)
                c = slice(slot * 1024, (slot + 1) * 1024)
                nc.scalar.copy(w_hi[:, c], w_raw[:, c]).then_inc(w_hi_done, 1)

            for n in range(4):
                c = slice(n * 2 * NT, (n + 1) * 2 * NT)
                act.wait_ge(x_in[n], 16)
                nc.scalar.copy(x_hi[:, c], x_raw[:, c]).then_inc(x_hi_done, 1)
                if n < 2:
                    split_hi(n, 1, None)

            with act.Fori(0, NHP) as m:
                for j in range(2):
                    act.wait_ge(pj_a_done, 2 * m + j + 1)
                    nc.scalar.copy(qk[:, bass.ds((2 * m + j) * NT, HALF)], pj_a[:, 0:HALF]).then_inc(qkv_a_read, 1)
                    split_hi(j, m + 2, 2 * m + j + 1)
            for f in range(NHP):
                t = 2 * NHP + f
                act.wait_ge(pj_a_done, t + 1)
                if f >= 2:
                    act.wait_ge(vt_done, f - 1)
                nc.scalar.copy(v_stage[f % 2][:, 0:HALF], pj_a[:, 0:HALF]).then_inc(qkv_a_read, 1)
                if f < 2:
                    split_hi(f, NHP + 2, t + 1)
                if f >= 1:
                    act.wait_ge(vt_done, f)
                    nc.scalar.copy(v_rows[:, :].rearrange("p (t n) -> p t n", t=QT)[:, :, (f - 1) * P:f * P],
                                   pt[:, :].rearrange("p (t n) -> p t n", t=QT)).then_inc(vt_read, 1)
            act.wait_ge(vt_done, NHP)
            nc.scalar.copy(v_rows[:, :].rearrange("p (t n) -> p t n", t=QT)[:, :, (NHP - 1) * P:],
                           pt[:, :].rearrange("p (t n) -> p t n", t=QT)).then_inc(vt_read, 1)

            def exp_prompt(i, u):
                w = (UNIT_ORDER[u][1] + 1) * P
                act.wait_ge(pr_masked, 1 + UNITS * i + u + 1)
                p = p_pr[:, u % 2 * 512:u % 2 * 512 + w]
                nc.scalar.activation(p, p, ACT.Exp, bias=negmax_pr[:, u % 2:u % 2 + 1], scale=-1.0,
                                     accum_out=sum_pr[:, u % 2:u % 2 + 1]).then_inc(pr_exp, 1)

            def move_prompt(i, u):
                w = (UNIT_ORDER[u][1] + 1) * P
                act.wait_ge(pr_turned, 1 + UNITS * i + u + 1)
                act.wait_ge(pr_pv, 1 + UNITS * i + max(0, u - 1))
                nc.scalar.copy(pt_pr[:, u % 2 * 512:u % 2 * 512 + w], pt[:, 0:w]).then_inc(pr_moved, 1)

            def exp_gate(i, tile, bank_, done, c0):
                act.wait_ge(done, QKV_TILES + ROUND_TILES * i + tile + 1)
                act.wait_ge(mixed, 1 + 4 * i + (0 if tile == 3 else 1 + c0 // HALF))
                nc.scalar.activation(rg[:, c0:c0 + HALF], bank_[:, 0:HALF], ACT.Exp, scale=-1.0).then_inc(g_exp, 1)

            with act.Fori(0, NPAIR) as i:
                t0 = QKV_TILES + ROUND_TILES * i
                in0 = QKV_TILES // 2 + 3 * i
                in1 = QKV_TILES // 2 + 2 * i
                split_hi(0, in0 + 1, t0)
                split_hi(1, in1 + 1, t0)
                for u in range(UNITS):
                    exp_prompt(i, u)
                    if u == 4:
                        act.wait_ge(s_max, i + 1)
                        nc.scalar.activation(p_s[:, :], p_s[:, :], ACT.Exp, bias=negmax_s, scale=-1.0,
                                             accum_out=sum_s).then_inc(s_exp, 1)
                        act.wait_ge(pj_a_done, t0 + 1)
                        act.wait_ge(u_done, 1 + 3 * i)
                        nc.scalar.copy(gcs[:, 0:HALF], pj_a[:, 0:HALF]).then_inc(c_read[0], 1)
                    if u == 5:
                        act.wait_ge(pj_b_done, t0 + 1)
                        nc.scalar.copy(gcs[:, HALF:], pj_b[:, 0:HALF]).then_inc(c_read[1], 1)
                    move_prompt(i, u)
                    if u == 5:
                        split_hi(0, in0 + 2, t0 + 1)
                split_hi(1, in1 + 2, t0 + 2)
                act.wait_ge(pr_pv, 1 + UNITS * (i + 1))
                act.wait_ge(mixed, 1 + 4 * i)
                nc.scalar.copy(o_pr[:, :], po[:, :]).then_inc(pr_out, 1)
                for g in range(2):
                    act.wait_ge(s_turned, 1 + 3 * i + g + 1)
                    if g == 0:
                        act.wait_ge(s_pv, 1 + i)
                    nc.scalar.copy(pt_s[:, g * 512:(g + 1) * 512], pt[:, :]).then_inc(s_moved, 1)
                split_hi(0, in0 + 3, t0 + 3)
                exp_gate(i, 3, pj_a, pj_a_done, 0)
                act.wait_ge(s_turned, 1 + 3 * i + 3)
                nc.scalar.copy(pt_s[:, 1024:1280], pt[:, 0:256]).then_inc(s_moved, 1)
                nc.scalar.copy(pt_s[0:NS, 1280:1408], pt[0:NS, 256:384]).then_inc(s_moved, 1)
                act.wait_ge(s_pv, 1 + i + 1)
                act.wait_ge(so_turned, 1 + i)
                nc.scalar.copy(o_s[:, :], po[:, :]).then_inc(s_out, 1)
                exp_gate(i, 3, pj_b, pj_b_done, HALF)
                act.wait_ge(so_turned, 1 + i + 1)
                for e in range(2):
                    dst = att_s[e * 64:e * 64 + 64, :].rearrange("p (h t) -> p h t", t=NS)[
                        :, :, bass.ds(16 * i, 16)].rearrange("p h (b q) -> p h b q", b=2)
                    nc.scalar.copy(dst, diagonal_ap(e)).then_inc(so_moved, 1)
                exp_gate(i, 4, pj_a, pj_a_done, 0)
                exp_gate(i, 4, pj_b, pj_b_done, HALF)

            act.wait_ge(kv_out, 48)
            act.wait_ge(s_pv, 1 + NPAIR)
            act.wait_ge(pj_b_done, W_TILES)
            for k in range(KT):
                loaded = QKV_TILES // 2 + (3, 2)[k % 2] * NPAIR + k // 2 + 1
                act.wait_ge(w_in[k % 2], 16 * loaded)
                nc.scalar.copy(wo[:, k * 2048:k * 2048 + 1024],
                               w_raw[:, k % 2 * 1024:(k % 2 + 1) * 1024]).then_inc(wo_hi_done, 1)
            act.wait_ge(mixed, 1 + 4 * NPAIR + 1)
            for k in range(KT):
                nc.scalar.copy(x_hi[:, k * NT:(k + 1) * NT], mix[:, k * NT:(k + 1) * NT]).then_inc(m_hi_done, 1)
            for t in range(QT + 1):
                rows = P if t < QT else NS
                act.wait_ge(ln_step, 6 * t + 4)
                nc.scalar.activation(std[0:rows, :], rstd[0:rows, :], ACT.Sqrt).then_inc(ln_sqrt, 1)

        @block.vector
        def _(dve):
            for opened in (pr_masked, s_masked, mixed, u_done, y_done):
                dve.sem_inc(opened, 1)

            def split_lo(slot, n):
                dve.wait_ge(w_hi_done, n)
                c = slice(slot * 1024, (slot + 1) * 1024)
                nc.vector.tensor_tensor(w_lo[:, c], w_raw[:, c], w_hi[:, c].bitcast(F32), ALU.subtract)\
                    .then_inc(w_lo_done, 1)

            for n in range(4):
                c = slice(n * 2 * NT, (n + 1) * 2 * NT)
                dve.wait_ge(x_hi_done, n + 1)
                nc.vector.tensor_tensor(x_lo[:, c], x_raw[:, c], x_hi[:, c].bitcast(F32), ALU.subtract)\
                    .then_inc(x_lo_done, 1)
                if n < 2:
                    split_lo(n, n + 1)

            with dve.Fori(0, NHP) as m:
                for j in range(2):
                    dve.wait_ge(pj_b_done, 2 * m + j + 1)
                    nc.vector.tensor_copy(qk[:, bass.ds((2 * m + j) * NT + HALF, HALF)], pj_b[:, 0:HALF])\
                        .then_inc(qkv_b_read, 1)
                    split_lo(j, 2 * m + j + 3)
            for f in range(NHP):
                t = 2 * NHP + f
                dve.wait_ge(pj_b_done, t + 1)
                if f >= 2:
                    dve.wait_ge(vt_done, f - 1)
                nc.vector.tensor_copy(v_stage[f % 2][:, HALF:], pj_b[:, 0:HALF]).then_inc(qkv_b_read, 1)
                if f < 2:
                    split_lo(f, t + 3)
                if f >= 1:
                    dve.wait_ge(vt_done, f)
                    nc.vector.tensor_copy(v_new[:, (f - 1) * P:f * P], po[0:NS, 0:P]).then_inc(vn_read, 1)
            dve.wait_ge(vt_done, NHP)
            nc.vector.tensor_copy(v_new[:, (NHP - 1) * P:], po[0:NS, 0:P]).then_inc(vn_read, 1)
            dve.wait_ge(small_in, 96)

            def mask_prompt(i, u):
                t = UNIT_ORDER[u][1]
                w = (t + 1) * P
                dve.wait_ge(small_in, 96)
                dve.wait_ge(pr_turned, 1 + UNITS * i + max(0, u - 1))
                dve.wait_ge(pr_scores, UNITS * i + u + 1)
                dve.sem_inc(may_mask, 1)
                nc.vector.tensor_tensor_reduce(
                    out=p_pr[:, u % 2 * 512:u % 2 * 512 + w], in0=px[:, 0:w], in1=mask_pr[:, SEQ - w:],
                    scale=-SCALE, scalar=BIG, op0=ALU.add, op1=ALU.min,
                    accum_out=negmax_pr[:, u % 2:u % 2 + 1]).then_inc(pr_masked, 1)

            def norm_prompt(i, u):
                w = (UNIT_ORDER[u][1] + 1) * P
                s = slice(u % 2, u % 2 + 1)
                dve.wait_ge(pr_exp, UNITS * i + u + 1)
                nc.vector.reciprocal(inv_pr[:, s], sum_pr[:, s]).then_inc(pr_inv, 1)
                dve.wait_ge(pr_inv, UNITS * i + u + 1)
                p = p_pr[:, u % 2 * 512:u % 2 * 512 + w]
                nc.vector.tensor_scalar(p, p, inv_pr[:, s], None, ALU.mult).then_inc(pr_norm, 1)

            def gate_half(i, tile, bank_, h):
                c = slice(h * HALF, (h + 1) * HALF)
                n = 2 * (tile - 3) + h
                dve.wait_ge(g_exp, 4 * i + n + 1)
                step = 12 * i + 3 * n
                nc.vector.tensor_scalar(rg[:, c], rg[:, c], 1.0, None, ALU.add).then_inc(g_step, 1)
                dve.wait_ge(g_step, step + 1)
                nc.vector.reciprocal(rg[:, c], rg[:, c]).then_inc(g_step, 1)
                dve.wait_ge(g_step, step + 2)
                if tile == 3:
                    nc.vector.tensor_tensor(rg[:, c], rg[:, c], zb[:, c], ALU.mult).then_inc(g_step, 1)
                else:
                    if h == 0:
                        dve.wait_ge(pr_out, i + 1)
                    e = slice(h * HALF, min((h + 1) * HALF, SEQ))
                    nc.vector.tensor_tensor(rg[:, e], rg[:, e], o_pr[:, e], ALU.mult).then_inc(g_step, 1)
                dve.wait_ge(g_step, step + 3)
                row = (NHP if tile == 3 else 0) + i
                nc.vector.tensor_tensor(mix[:, bass.ds(row * NT + h * HALF, HALF)], bank_[:, 0:HALF], rg[:, c],
                                        ALU.mult).then_inc(mixed, 1)

            with dve.Fori(0, NPAIR) as i:
                t0 = QKV_TILES + ROUND_TILES * i
                split_lo(0, t0 + 1)
                split_lo(1, t0 + 2)
                for u in range(UNITS):
                    mask_prompt(i, u)
                    norm_prompt(i, u)
                    if u == 3:
                        dve.wait_ge(small_in, 96)
                        dve.wait_ge(k_used, 1 + 4 * i + 4)
                        dve.wait_ge(masked_new, i + 1)
                        dve.wait_ge(s_turned, 1 + 3 * i)
                        dve.sem_inc(may_mask, 1)
                        for c, (c0, w) in enumerate(CHUNKS):
                            w = w + (NS if c == 2 else 0)
                            nc.vector.tensor_tensor_reduce(
                                out=p_s[:, c0:c0 + w], in0=sc[c][:, 0:w], in1=mask_s[:, c0:c0 + w],
                                scale=-SCALE, scalar=BIG, op0=ALU.add, op1=ALU.min,
                                accum_out=negmax3[:, c:c + 1]).then_inc(s_masked, 1)
                        dve.wait_ge(s_masked, 1 + 3 * i + 3)
                        nc.vector.tensor_reduce(negmax_s, negmax3, AX_X, ALU.min).then_inc(s_max, 1)
                    if u == 4:
                        dve.wait_ge(s_exp, i + 1)
                        nc.vector.reciprocal(inv_s, sum_s).then_inc(s_inv, 1)
                        dve.wait_ge(s_inv, i + 1)
                        nc.vector.tensor_scalar(p_s[:, :], p_s[:, :], inv_s, None, ALU.mult).then_inc(s_norm, 1)
                    if u == 6:
                        dve.wait_ge(pj_a_done, t0 + 2)
                        dve.wait_ge(padded, 2 * i + 2)
                        dve.wait_ge(c_read[0], i + 1)
                        nc.vector.tensor_tensor(u_pad[:, 2:2 + HALF], pj_a[:, 0:HALF], gcs[:, 0:HALF], ALU.mult)\
                            .then_inc(u_done, 1)
                        split_lo(0, t0 + 3)
                dve.wait_ge(pj_b_done, t0 + 2)
                dve.wait_ge(c_read[1], i + 1)
                nc.vector.tensor_tensor(u_pad[:, 2 + HALF:2 + SEQ], pj_b[:, 0:HP_LEFT], gcs[:, HALF:SEQ], ALU.mult)\
                    .then_inc(u_done, 1)
                nc.vector.tensor_tensor(u_s[:, :, 2:], pj_b[:, HP_LEFT:HALF].rearrange("p (b t) -> p b t", t=DEC_SEQ),
                                        gcs[:, SEQ:].rearrange("p (b t) -> p b t", t=DEC_SEQ), ALU.mult)\
                    .then_inc(u_done, 1)
                split_lo(1, t0 + 4)
                n = PAD_COLS - 2
                dve.wait_ge(u_done, 1 + 3 * i + 3)
                nc.vector.tensor_scalar(y_pad[:, 0:n], u_pad[:, 0:n], cw[:, 0:1], None, ALU.mult).then_inc(y_step, 1)
                dve.wait_ge(y_step, 2 * i + 1)
                nc.vector.scalar_tensor_tensor(y_pad[:, 0:n], u_pad[:, 1:n + 1], cw[:, 1:2], y_pad[:, 0:n],
                                               ALU.mult, ALU.add).then_inc(y_step, 1)
                dve.wait_ge(y_step, 2 * i + 2)
                nc.vector.scalar_tensor_tensor(y_pad[:, 0:n], u_pad[:, 2:n + 2], cw[:, 2:3], y_pad[:, 0:n],
                                               ALU.mult, ALU.add).then_inc(y_done, 1)
                dve.wait_ge(y_done, 1 + i + 1)
                dve.wait_ge(pj_a_done, t0 + 3)
                nc.vector.tensor_tensor(zb[:, 0:HALF], pj_a[:, 0:HALF], y_pad[:, 0:HALF], ALU.mult).then_inc(z_done, 1)
                dve.wait_ge(pj_b_done, t0 + 3)
                nc.vector.tensor_tensor(zb[:, HALF:SEQ], pj_b[:, 0:HP_LEFT], y_pad[:, HALF:SEQ], ALU.mult)\
                    .then_inc(z_done, 1)
                nc.vector.tensor_tensor(zb[:, SEQ:].rearrange("p (b t) -> p b t", t=DEC_SEQ),
                                        pj_b[:, HP_LEFT:HALF].rearrange("p (b t) -> p b t", t=DEC_SEQ),
                                        y_s[:, :, 0:DEC_SEQ], ALU.mult).then_inc(z_done, 1)
                split_lo(0, t0 + 5)
                dve.wait_ge(z_done, 3 * i + 3)
                gate_half(i, 3, pj_a, 0)
                gate_half(i, 3, pj_b, 1)
                gate_half(i, 4, pj_a, 0)
                gate_half(i, 4, pj_b, 1)

            dve.wait_ge(so_moved, 1 + 2 * NPAIR)
            dve.wait_ge(mixed, 1 + 4 * NPAIR)
            m = mix[:, 0:NHP * NT].rearrange("p (h t) -> p h t", t=NT)[:, :, SEQ:]
            nc.vector.tensor_tensor(m, m, att_s[:, :].rearrange("p (h t) -> p h t", t=NS), ALU.mult).then_inc(mixed, 1)
            for k in range(KT):
                dve.wait_ge(wo_hi_done, k + 1)
                nc.vector.tensor_tensor(wo[:, k * 2048 + 1024:(k + 1) * 2048], w_raw[:, k % 2 * 1024:(k % 2 + 1) * 1024],
                                        wo[:, k * 2048:k * 2048 + 1024].bitcast(F32), ALU.subtract)\
                    .then_inc(w_lo_done, 1)
            for k in range(KT):
                c = slice(k * NT, (k + 1) * NT)
                dve.wait_ge(m_hi_done, k + 1)
                nc.vector.tensor_tensor(x_lo[:, c], mix[:, c], x_hi[:, c].bitcast(F32), ALU.subtract)\
                    .then_inc(m_lo_done, 1)

            dve.wait_ge(ln_in, 32)
            for t in range(QT + 1):
                rows = P if t < QT else NS
                banks = (sc[0], sc[1]) if t % 2 == 0 else (sc[2], px)
                y = y_t[0:rows, t % 2 * 1024:(t % 2 + 1) * 1024]
                xr = x_res[0:rows, t % 2 * 1024:(t % 2 + 1) * 1024]
                step = 6 * t
                dve.wait_ge(res_in[t % 2], 16 * (t // 2 + 1))
                if t >= 2:
                    dve.wait_ge(y_out[t % 2], 16 * (t // 2))
                for h in range(2):
                    c = slice(h * 512, (h + 1) * 512)
                    dve.wait_ge(o_done, 2 * t + h + 1)
                    nc.vector.scalar_tensor_tensor(y[:, c], xr[:, c], ALPHA, banks[h][0:rows, :], ALU.mult, ALU.add)\
                        .then_inc(r_done, 1)
                for h in range(2):
                    dve.wait_ge(r_done, 2 * t + h + 1)
                    nc.vector.bn_stats(bn[0:rows, 6 * h:6 * h + 6], y[:, h * 512:(h + 1) * 512]).then_inc(ln_step, 1)
                dve.wait_ge(ln_step, step + 2)
                nc.vector.bn_aggr(mv[0:rows, :], bn[0:rows, :]).then_inc(ln_step, 1)
                dve.wait_ge(ln_step, step + 3)
                nc.vector.tensor_scalar(rstd[0:rows, :], mv[0:rows, 1:2], LN_EPS, None, ALU.add).then_inc(ln_step, 1)
                dve.wait_ge(ln_sqrt, t + 1)
                nc.vector.reciprocal(rstd[0:rows, :], std[0:rows, :]).then_inc(ln_step, 1)
                dve.wait_ge(ln_step, step + 5)
                nc.vector.tensor_scalar(y, y, mv[0:rows, 0:1], rstd[0:rows, :], ALU.subtract, ALU.mult)\
                    .then_inc(ln_step, 1)
                dve.wait_ge(ln_step, step + 6)
                nc.vector.tensor_tensor(y, y, ln_g[0:rows, :], ALU.mult).then_inc(ln_scaled, 1)
                dve.wait_ge(ln_scaled, t + 1)
                nc.vector.tensor_tensor(y, y, ln_b[0:rows, :], ALU.add).then_inc(ln_done, 1)

        @block.tensor
        def _(pe):
            def project(slot, tile, h, *reads):
                out = (pj_a, pj_b)[h]
                if h == 0:
                    pe.wait_ge(w_lo_done, tile + 1)
                for read, count in reads:
                    pe.wait_ge(read, count)
                for k in range(KT):
                    w = slice(slot * 1024 + k * P, slot * 1024 + (k + 1) * P)
                    c = slice(k * NT + h * HALF, k * NT + (h + 1) * HALF)
                    nc.tensor.matmul(out[:, 0:HALF], w_hi[:, w], x_hi[:, c], start=(k == 0), stop=False)
                    nc.tensor.matmul(out[:, 0:HALF], w_hi[:, w], x_lo[:, c], start=False, stop=False)
                    last = nc.tensor.matmul(out[:, 0:HALF], w_lo[:, w], x_hi[:, c], start=False, stop=(k == KT - 1))
                last.then_inc((pj_a_done, pj_b_done)[h], 1)

            def turn_v(f):
                pe.wait_ge(qkv_a_read, 2 * NHP + f + 1)
                pe.wait_ge(qkv_b_read, 2 * NHP + f + 1)
                if f == 0:
                    pe.wait_ge(small_in, 96)
                else:
                    pe.wait_ge(vt_read, f)
                    pe.wait_ge(vn_read, f)
                v = v_stage[f % 2]
                for t in range(QT):
                    nc.tensor.transpose(pt[:, t * P:(t + 1) * P], v[:, t * P:(t + 1) * P], ident[:, :])
                nc.tensor.transpose(po[0:NS, 0:P], v[:, SEQ:], ident[:, :]).then_inc(vt_done, 1)

            for opened in (k_used, v_used, pr_turned, pr_pv, s_turned, s_pv, so_turned):
                pe.sem_inc(opened, 1)
            pe.wait_ge(x_lo_done, 4)
            project(0, 0, 0)
            project(0, 0, 1)
            qkv_read = (qkv_a_read, qkv_b_read)
            project(1, 1, 0, (qkv_read[0], 1))
            project(1, 1, 1, (qkv_read[1], 1))
            with pe.Fori(1, NHP) as m:
                for j in range(2):
                    for h in range(2):
                        project(j, 2 * m + j, h, (qkv_read[h], 2 * m + j))
            for f in range(NHP):
                for h in range(2):
                    project(f % 2, 2 * NHP + f, h, (qkv_read[h], 2 * NHP + f))
                if f >= 1:
                    turn_v(f - 1)
            turn_v(NHP - 1)

            def prompt_scores(i, u):
                e, t = UNIT_ORDER[u]
                if u == 0:
                    pe.wait_ge(staged, 3 * i + 3)
                pe.wait_ge(pr_masked, 1 + UNITS * i + u)
                w = (t + 1) * P
                nc.tensor.matmul(px[:, 0:w], q_st[e * 64:e * 64 + 64, t * P:(t + 1) * P],
                                 k_st[e * 64:e * 64 + 64, 0:w], start=True, stop=True).then_inc(pr_scores, 1)

            def prompt_turn(i, u):
                t = UNIT_ORDER[u][1]
                pe.wait_ge(pr_norm, UNITS * i + u + 1)
                if u == 0:
                    pe.wait_ge(so_moved, 1 + 2 * i)
                    pe.wait_ge(vt_read, NHP)
                else:
                    pe.wait_ge(pr_moved, UNITS * i + u)
                for k in range(t + 1):
                    c = u % 2 * 512 + k * P
                    last = nc.tensor.transpose(pt[:, k * P:(k + 1) * P], p_pr[:, c:c + P], ident[:, :])
                last.then_inc(pr_turned, 1)

            def prompt_values(i, u):
                e, t = UNIT_ORDER[u]
                pe.wait_ge(pr_moved, UNITS * i + u + 1)
                if u == 0:
                    pe.wait_ge(s_out, 1 + i)
                    pe.wait_ge(vn_read, NHP)
                for k in range(t + 1):
                    last = nc.tensor.matmul(po[e * 64:e * 64 + 64, t * P:(t + 1) * P],
                                            v_st[:, k * P + e * 64:k * P + e * 64 + 64],
                                            pt_pr[:, u % 2 * 512 + k * P:u % 2 * 512 + (k + 1) * P],
                                            start=(k == 0), stop=(k == t))
                last.then_inc(pr_pv, 1)

            def sample_scores(i, hp):
                pe.wait_ge(k_in[hp % 2], 16 * (2 * i + hp // 2 + 1))
                if hp == 0:
                    pe.wait_ge(qbd_done, 2 * i + 2)
                    pe.wait_ge(s_masked, 1 + 3 * i)
                for c, (c0, w) in enumerate(CHUNKS):
                    for b in range(2):
                        rows = slice(b * 64, b * 64 + 64)
                        q = q_bd[:, hp * P + b * 64:hp * P + b * 64 + 64]
                        k0 = hp % 2 * 2560 + b * USED + c0
                        last = nc.tensor.matmul(sc[c][rows, 0:w], q, k_buf[:, k0:k0 + w], start=(hp == 0),
                                                stop=(hp == NHP - 1 and c < 2), skip_group_check=True)
                        if c == 2:
                            last = nc.tensor.matmul(sc[c][rows, w:w + NS], q,
                                                    qk[:, (NHP + hp) * NT + SEQ:(NHP + hp + 1) * NT],
                                                    start=False, stop=(hp == NHP - 1), skip_group_check=True)
                last.then_inc(k_used, 1)

            def sample_turn(i, g):
                if g == 0:
                    pe.wait_ge(s_norm, i + 1)
                    pe.wait_ge(pr_moved, UNITS * (i + 1))
                else:
                    pe.wait_ge(s_moved, 4 * i + g)
                tiles = range(4 * g, min(4 * g + 4, USED_TILES))
                for n, t in enumerate(tiles):
                    last = nc.tensor.transpose(pt[:, n * P:(n + 1) * P], p_s[:, t * P:(t + 1) * P], ident[:, :])
                if g == 2:
                    last = nc.tensor.transpose(pt[0:NS, 256:384], p_s[:, USED:], ident[:, :])
                last.then_inc(s_turned, 1)

            def sample_values(i):
                pe.wait_ge(s_moved, 4 * i + 4)
                pe.wait_ge(pr_out, i + 1)
                for s in range(V_PIECES // 2):
                    for b in range(2):
                        n = 2 * s + b
                        pe.wait_ge(v_in[n % V_SLOTS], 16 * (2 * i + n // V_SLOTS + 1))
                    for half in range(2):
                        for b in range(2):
                            n = 2 * s + b
                            t = 2 * s + half
                            v0 = n % V_SLOTS * 1024 + half * 512
                            last = nc.tensor.matmul(po[b * 64:b * 64 + 64, :],
                                                    pt_s[:, t * P + b * 64:t * P + b * 64 + 64],
                                                    v_buf[:, v0:v0 + 512], start=(t == 0), stop=False)
                            if half == 1:
                                last.then_inc(v_used, 1)
                for b in range(2):
                    last = nc.tensor.matmul(po[b * 64:b * 64 + 64, :],
                                            pt_s[0:NS, USED + b * 64:USED + b * 64 + 64],
                                            v_new[:, :], start=False, stop=True)
                last.then_inc(s_pv, 1)

            def sample_out_turn(i):
                pe.wait_ge(s_out, 1 + i + 1)
                for hp in range(NHP):
                    last = nc.tensor.transpose(pt[:, hp * P:(hp + 1) * P], o_s[:, hp * P:(hp + 1) * P], ident[:, :])
                last.then_inc(so_turned, 1)

            with pe.Fori(0, NPAIR) as i:
                t0 = QKV_TILES + ROUND_TILES * i
                for u in range(UNITS):
                    prompt_scores(i, u)
                    if u < NHP:
                        sample_scores(i, u)
                    else:
                        h = u % 2
                        if u < NHP + 2:
                            project(0, t0, h, (mixed, 1 + 4 * i), (qkv_read[h], QKV_TILES))
                        else:
                            project(1, t0 + 1, h, (c_read[h], i + 1))
                    prompt_turn(i, u)
                    if u:
                        prompt_values(i, u - 1)
                project(0, t0 + 2, 0, (u_done, 1 + 3 * i + 1))
                prompt_values(i, UNITS - 1)
                sample_turn(i, 0)
                project(0, t0 + 2, 1, (u_done, 1 + 3 * i + 3))
                sample_turn(i, 1)
                project(1, t0 + 3, 0, (z_done, 3 * i + 1))
                sample_turn(i, 2)
                sample_values(i)
                project(1, t0 + 3, 1, (z_done, 3 * i + 3))
                sample_out_turn(i)
                project(0, t0 + 4, 0, (mixed, 1 + 4 * i + 1))
                project(0, t0 + 4, 1, (mixed, 1 + 4 * i + 2))

            pe.wait_ge(s_masked, 1 + 3 * NPAIR)
            pe.wait_ge(pr_masked, 1 + UNITS * NPAIR)
            for t in range(QT + 1):
                rows = P if t < QT else NS
                banks = (sc[0], sc[1]) if t % 2 == 0 else (sc[2], px)
                if t >= 2:
                    pe.wait_ge(r_done, 2 * (t - 1))
                for k in range(KT):
                    if t == 0:
                        pe.wait_ge(w_lo_done, W_TILES + k + 1)
                        pe.wait_ge(m_lo_done, k + 1)
                    tok = slice(k * NT + t * P, k * NT + t * P + rows)
                    for h in range(2):
                        hi = slice(k * 2048 + h * 512, k * 2048 + (h + 1) * 512)
                        lo = slice(k * 2048 + 1024 + h * 512, k * 2048 + 1024 + (h + 1) * 512)
                        out = banks[h][0:rows, :]
                        nc.tensor.matmul(out, x_hi[:, tok], wo[:, hi], start=(k == 0), stop=False)
                        nc.tensor.matmul(out, x_hi[:, tok], wo[:, lo], start=False, stop=False)
                        last = nc.tensor.matmul(out, x_lo[:, tok], wo[:, hi], start=False, stop=(k == KT - 1))
                        if k == KT - 1:
                            last.then_inc(o_done, 1)



def log_count(distance):
    d = np.asarray(distance)
    count = sum(((d >= 0) & (d <= w) & (d % r == 0)).astype(np.int64) for w, r in PAIRS)
    return np.where(count > 0, np.log(np.maximum(count, 1)), NEG)


def mask_arrays():
    p = np.arange(P)
    cached = np.empty((USED_TILES, P), np.int64)
    for r in range(8):
        cached[r] = 16 * p + r
    for s in range(2):
        cached[8 + s] = PAST_LEN - 512 + 16 * (p % 32) + 8 + 2 * (p // 32) + s
    row = np.arange(P)
    batch, query = row // 64, row % DEC_SEQ
    mask_s = log_count(PAST_LEN + query[:, None] - cached.reshape(1, -1))
    col = np.arange(NS)
    new = []
    for pair in range(NPAIR):
        m = log_count(query[:, None] - col[None, :] % DEC_SEQ)
        new.append(np.where(col[None, :] // DEC_SEQ == 2 * pair + batch[:, None], m, NEG))
    mask_pr = log_count(p[:, None] + SEQ - P - np.arange(SEQ)[None, :])
    scaled = [np.maximum(m / SCALE, NEG).astype(np.float32) for m in (mask_s, np.concatenate(new, 1), mask_pr)]
    return dict(zip(("mask_s", "mask_new", "mask_pr"), scaled))



def split_cache(c):
    c = np.asarray(c).reshape(DEC_BATCH, P, 16, D_ATT)
    old = c[:, :, 0:8].transpose(0, 2, 1, 3)
    recent = c[:, 96:, 8:].reshape(DEC_BATCH, 32, 4, 2, D_ATT).transpose(0, 3, 2, 1, 4)
    return np.concatenate([old, recent.reshape(DEC_BATCH, 2, P, D_ATT)], 1), c[:, :96, 8:]


def join_cache(used, rest, new):
    c = np.empty((DEC_BATCH, P, 16, D_ATT), np.float32)
    c[:, :, 0:8] = used[:, 0:8].transpose(0, 2, 1, 3)
    c[:, 96:, 8:] = used[:, 8:].reshape(DEC_BATCH, 2, 4, 32, D_ATT).transpose(0, 3, 2, 1, 4)\
        .reshape(DEC_BATCH, 32, 8, D_ATT)
    c[:, :96, 8:] = rest.reshape(DEC_BATCH, 96, 8, D_ATT)
    c = np.concatenate([c.reshape(DEC_BATCH, PAST_LEN, D_ATT)[:, DEC_SEQ:], new], 1)
    return c.reshape(DEC_BATCH, PAST_LEN, N_HEADS, HEAD_DIM)


def kernel(x_prompt, x_sample, cache_k, cache_v, state_conv, w_in, conv_w, w_out, ln_g, ln_b):
    import concourse.bacc as bacc
    from concourse.bass_utils import run_bass_kernel_spmd

    a = {}
    x = np.concatenate([np.asarray(x_prompt).reshape(SEQ, D_MODEL), np.asarray(x_sample).reshape(NS, D_MODEL)])
    a["x_rows"] = x
    a["xT"] = x.reshape(NT, KT, P).transpose(2, 1, 0).reshape(P, KT * NT)
    order = list(range(QKV_TILES)) + [NHP * g + i for i in range(NPAIR) for g in (5, 6, 4, 7, 3)]
    w = np.asarray(w_in).reshape(KT, P, 32, P).transpose(2, 1, 0, 3)[order].reshape(32 * P, 1024)
    a["w_tiles"] = np.concatenate([w, np.asarray(w_out)])
    k_used, k_rest = split_cache(cache_k)
    v_used, v_rest = split_cache(cache_v)
    a["k_used"] = k_used.reshape(NPAIR, 2, USED, NHP, P).transpose(0, 3, 4, 1, 2).reshape(NPAIR * NHP * P, 2 * USED)
    a["v_used"] = v_used.reshape(NPAIR, 2, 5, 2, P, D_ATT).transpose(0, 2, 1, 4, 3, 5).reshape(NPAIR * 10 * P, 1024)
    a["k_rest"], a["v_rest"] = (r.reshape(REST_ROWS * 256, 1024) for r in (k_rest, v_rest))
    a["state"] = np.asarray(state_conv).reshape(DEC_BATCH, 2, NHP, P).transpose(3, 2, 0, 1).reshape(P, -1)
    a["conv_w"] = np.asarray(conv_w).reshape(CONV_WIDTH, NHP, P).transpose(2, 1, 0).reshape(P, -1)
    a["ln_g"], a["ln_b"] = np.asarray(ln_g).reshape(1, -1), np.asarray(ln_b).reshape(1, -1)
    a["ident"] = np.eye(P, dtype=np.float32)
    a.update(mask_arrays())
    a = {name: np.ascontiguousarray(v) for name, v in a.items()}
    outs = {
        "y": (NT, D_MODEL), "kT_new": (P, NHP * NT), "v_prompt": (SEQ, D_ATT), "v_sample": (NS, D_ATT),
        "new_conv": (P, NHP * 18),
        **{name + "_out": a[name].shape for name in ("k_used", "v_used", "k_rest", "v_rest")},
    }
    nc = bacc.Bacc("TRN2", target_bir_lowering=False, num_devices=1)
    d = {n: nc.dram_tensor("in_" + n, v.shape, F32, kind="ExternalInput").ap() for n, v in a.items()}
    d.update({n: nc.dram_tensor("out_" + n, s, F32, kind="ExternalOutput").ap() for n, s in outs.items()})
    layer_step(nc, d)
    got = run_bass_kernel_spmd(nc, [{"in_" + n: v for n, v in a.items()}], core_ids=[0]).results[0]
    r = {n: got["out_" + n] for n in outs}

    y = r["y"]
    k_rows = r["kT_new"].reshape(P, NHP, NT).transpose(2, 1, 0).reshape(NT, D_ATT)
    k_used = r["k_used_out"].reshape(NPAIR, NHP, P, 2, USED_TILES, P).transpose(0, 3, 4, 5, 1, 2)\
        .reshape(DEC_BATCH, USED_TILES, P, D_ATT)
    v_used = r["v_used_out"].reshape(NPAIR, 5, 2, P, 2, D_ATT).transpose(0, 2, 1, 4, 3, 5)\
        .reshape(DEC_BATCH, USED_TILES, P, D_ATT)
    conv = r["new_conv"].reshape(P, NHP, 18).transpose(2, 1, 0).reshape(18, D_ATT)
    prompt = (1, SEQ, N_HEADS, HEAD_DIM)
    return (
        y[:SEQ].reshape(1, SEQ, D_MODEL),
        y[SEQ:].reshape(DEC_BATCH, DEC_SEQ, D_MODEL),
        k_rows[:SEQ].reshape(prompt),
        r["v_prompt"].reshape(prompt),
        conv[:2].reshape(1, 2, D_ATT),
        join_cache(k_used, r["k_rest_out"], k_rows[SEQ:].reshape(DEC_BATCH, DEC_SEQ, D_ATT)),
        join_cache(v_used, r["v_rest_out"], r["v_sample"].reshape(DEC_BATCH, DEC_SEQ, D_ATT)),
        conv[2:].reshape(DEC_BATCH, 2, D_ATT),
    )
```

```python
from contextlib import ExitStack

import numpy as np

import concourse.bass as bass
from concourse import mybir

P = 128
D_MODEL = 1024
SEQ = 512
DEC_BATCH = 8
DEC_SEQ = 8
PAST_LEN = 2048
N_HEADS = 8
HEAD_DIM = 64
D_ATT = N_HEADS * HEAD_DIM
CONV_WIDTH = 3
PAIRS = ((128, 1), (512, 4), (2048, 16))
LN_EPS = 1e-5
ALPHA = 2.0 ** 0.25
SCALE = HEAD_DIM ** -0.5

NS = DEC_BATCH * DEC_SEQ
NT = SEQ + NS
HALF = NT // 2
HP_LEFT = SEQ - HALF
KT = D_MODEL // P
NHP = D_ATT // P
NPAIR = DEC_BATCH // 2
QKV_TILES = 3 * NHP
ROUND_TILES = 5
W_TILES = QKV_TILES + NPAIR * ROUND_TILES
USED_TILES = 10
USED = USED_TILES * P
REST = PAST_LEN - USED
REST_ROWS = DEC_BATCH * REST * D_ATT // (256 * 1024)
S_COLS = USED + NS
V_PIECES = 10
V_SLOTS = 5
QT = SEQ // P
UNITS = 2 * QT
UNIT_ORDER = [(e, t) for t in reversed(range(QT)) for e in range(2)]
X_CHUNKS = ((0, 1), (1, 3), (3, 5), (5, 7), (7, 8))
CHUNKS = ((0, 512), (512, 512), (1024, 256))
PAD_COLS = 2 + SEQ + DEC_BATCH * (2 + DEC_SEQ)
NEG = -1e30
BIG = 3e38

F32 = mybir.dt.float32
F32R = mybir.dt.float32r
ALU = mybir.AluOpType
ACT = mybir.ActivationFunctionType
AX_X = mybir.AxisListType.X


LATE_COPIES = NPAIR - 1 + 2 * (REST_ROWS - NHP - 3)
MIX_ORDER = (4, 5, 6, 7, 0, 1, 2, 3)
MIX_SPLITS = [(4 * NPAIR - 2, NHP, 2 * NHP, 0, P), (4 * NPAIR - 1, 0, NHP, 0, P)] + [
    (4 * NPAIR - ((t + 1) * P <= HALF), 0, 2 * NHP, t * P, (t + 1) * P) for t in range(1, QT)] + [(4 * NPAIR + 1, 0, 2 * NHP, SEQ, NT)]


def token_cols(features, k0, k1, c0, c1):
    return features[:, k0 * NT:k1 * NT].rearrange("p (k t) -> p k t", t=NT)[:, :, c0:c1]


def layer_step(nc, d):
    with ExitStack() as ctx:
        def sb(name, shape, dt=F32, stack=ctx):
            return stack.enter_context(nc.sbuf_tensor(name, shape, dt))

        def bank(name):
            return ctx.enter_context(nc.psum_tensor(name, [P, 512], F32))

        def sem(name):
            return ctx.enter_context(nc.semaphore(name))

        x_hi = sb("x_hi", [P, KT * NT], F32R)
        x_lo = sb("x_lo", [P, KT * NT], F32R)
        w_raw = sb("w_raw", [P, 2 * 1024])
        w_hi = sb("w_hi", [P, 2 * 1024], F32R)
        w_lo = sb("w_lo", [P, 2 * 1024], F32R)
        mix = sb("mix", [P, 2 * NHP * NT])
        gcs = sb("gcs", [P, NT])
        zb = sb("zb", [P, NT])
        rg = sb("rg", [P, NT])
        u_pad = sb("u_pad", [P, PAD_COLS])
        y_pad = sb("y_pad", [P, PAD_COLS])
        att_s = sb("att_s", [P, NHP * NS])
        new_conv = sb("new_conv", [P, NHP * 2 * (1 + DEC_BATCH)])
        state = sb("state", [P, NHP * 2 * DEC_BATCH])
        conv_w = sb("conv_w", [P, NHP * CONV_WIDTH])
        cw = sb("cw", [P, CONV_WIDTH])
        ident = sb("ident", [P, P])
        stat = sb("stat", [P, 48])
        early = ctx.enter_context(ExitStack())
        k_buf = sb("k_buf", [P, 2 * 2560], stack=early)
        qk = sb("qk", [P, 2 * NHP * NT], stack=early)
        v_rows = sb("v_rows", [P, QT * D_ATT], stack=early)
        q_st = sb("q_st", [P, SEQ], stack=early)
        k_st = sb("k_st", [P, SEQ], stack=early)
        v_st = sb("v_st", [P, SEQ], stack=early)
        p_pr = sb("p_pr", [P, 2 * 512], stack=early)
        pt_pr = sb("pt_pr", [P, 2 * 512], stack=early)
        mask_s = sb("mask_s", [P, S_COLS], stack=early)
        p_s = sb("p_s", [P, S_COLS], stack=early)
        v_new = sb("v_new", [NS, D_ATT], stack=early)
        v_buf = sb("v_buf", [P, V_SLOTS * 1024], stack=early)
        pt_s = sb("pt_s", [P, (USED_TILES + 1) * P], stack=early)
        o_s = sb("o_s", [P, D_ATT], stack=early)
        o_pr = sb("o_pr", [P, SEQ], stack=early)
        mask_new = sb("mask_new", [P, NPAIR * NS], stack=early)
        mask_pr = sb("mask_pr", [P, SEQ], stack=early)
        q_bd = sb("q_bd", [P, NHP * P], stack=early)
        early.close()
        as_loaded = ctx.enter_context(ExitStack())
        wo_raw = sb("wo_raw", [P, KT * 2 * 1024], stack=as_loaded)
        as_loaded.close()
        wo = sb("wo", [P, KT * 2 * 1024], F32R)
        ln_g = sb("ln_g", [P, D_MODEL])
        ln_b = sb("ln_b", [P, D_MODEL])
        x_res = sb("x_res", [P, 2 * D_MODEL])
        y_t = sb("y_t", [P, 2 * D_MODEL])

        pj_a, pj_b = bank("pj_a"), bank("pj_b")
        sc = [bank(f"sc{c}") for c in range(3)]
        px, pt, po = bank("px"), bank("pt"), bank("po")

        x_in = [sem(f"x_in{n}") for n in range(len(X_CHUNKS))]
        small_in, ln_in, ln_spread = sem("small_in"), sem("ln_in"), sem("ln_spread")
        res_in = [sem("res_in0"), sem("res_in1")]
        wo_in = [sem(f"wo_in{n}") for n in range(KT)]
        w_in = [sem("w_in0"), sem("w_in1")]
        k_in = [sem("k_in0"), sem("k_in1")]
        v_in = [sem(f"v_in{n}") for n in range(V_SLOTS)]
        kv_out, copied, conv_out = sem("kv_out"), sem("copied"), sem("conv_out")
        y_out = [sem("y_out0"), sem("y_out1")]
        x_hi_done, x_lo_done = sem("x_hi_done"), sem("x_lo_done")
        w_hi_done, w_lo_done = sem("w_hi_done"), sem("w_lo_done")
        pj_a_done, pj_b_done = sem("pj_a_done"), sem("pj_b_done")
        qkv_a_read, qkv_b_read = sem("qkv_a_read"), sem("qkv_b_read")
        c_read = [sem("c_read_a"), sem("c_read_b")]
        vt_done, vt_read, vn_read = sem("vt_done"), sem("vt_read"), sem("vn_read")
        staged, zeroed, qbd_done, masked_new, padded = (
            sem("staged"), sem("zeroed"), sem("qbd_done"), sem("masked_new"), sem("padded"))
        u_done, y_done, z_done, new_conv_done = sem("u_done"), sem("y_done"), sem("z_done"), sem("new_conv_done")
        v_staged = sem("v_staged")
        y_step, may_mask = sem("y_step"), sem("may_mask")
        k_used, v_used = sem("k_used"), sem("v_used")
        pr_scores, pr_masked, pr_exp, pr_inv, pr_norm = (
            sem("pr_scores"), sem("pr_masked"), sem("pr_exp"), sem("pr_inv"), sem("pr_norm"))
        pr_turned, pr_moved, pr_pv, pr_out = sem("pr_turned"), sem("pr_moved"), sem("pr_pv"), sem("pr_out")
        s_masked, s_max, s_exp, s_inv, s_norm = (
            sem("s_masked"), sem("s_max"), sem("s_exp"), sem("s_inv"), sem("s_norm"))
        s_turned, s_moved, s_pv, s_out = sem("s_turned"), sem("s_moved"), sem("s_pv"), sem("s_out")
        so_turned, so_moved = sem("so_turned"), sem("so_moved")
        g_exp, g_step, mixed = sem("g_exp"), sem("g_step"), sem("mixed")
        m_hi_done, m_lo_done, wo_hi_done, wo_lo_done = (
            sem("m_hi_done"), sem("m_lo_done"), sem("wo_hi_done"), sem("wo_lo_done"))
        o_done, r_done, ln_step, ln_sqrt, ln_scaled, ln_done = (
            sem("o_done"), sem("r_done"), sem("ln_step"), sem("ln_sqrt"), sem("ln_scaled"), sem("ln_done"))

        x_raw = k_buf[:, 0:KT * NT]
        v_stage = [gcs, zb]
        u_s = u_pad[:, 2 + SEQ:].rearrange("p (b t) -> p b t", t=2 + DEC_SEQ)
        y_s = y_pad[:, 2 + SEQ:].rearrange("p (b t) -> p b t", t=2 + DEC_SEQ)
        negmax_pr, sum_pr, inv_pr = stat[:, 0:2], stat[:, 2:4], stat[:, 4:6]
        negmax3, negmax_s, sum_s, inv_s = stat[:, 6:9], stat[:, 9:10], stat[:, 10:11], stat[:, 11:12]
        bn, mv, rstd = stat[:, 12:24], stat[:, 24:26], stat[:, 26:27]
        std = stat[:, 27:28]

        def qbd_copy_ap(e):
            a = q_bd[e * 64:e * 64 + 64, e * 8:e * 8 + 8]
            return bass.AP(tensor=a.tensor, offset=a.offset, ap=[[NHP * P, 64], [P + 16, NHP], [64, 2], [1, 8]])

        def diagonal_ap(e):
            a = pt[e * 64:e * 64 + 64, e * 8:e * 8 + 8]
            return bass.AP(tensor=a.tensor, offset=a.offset, ap=[[512, 64], [P + 16, NHP], [64, 2], [1, 8]])

        block = ctx.enter_context(nc.Block())

        @block.sync
        def _(sp):
            def load_w(tile, slot, split_before):
                if split_before is not None:
                    sp.wait_ge(w_lo_done, split_before)
                sp.dma_start(w_raw[:, slot * 1024:(slot + 1) * 1024],
                             d["w_tiles"][bass.ds(tile * P, P), :]).then_inc(w_in[slot], 16)

            def load_k(i, hp):
                sp.wait_ge(k_used, NHP * i + hp + 1)
                sp.dma_start(k_buf[:, hp % 2 * 2560:(hp % 2 + 1) * 2560],
                             d["k_used"][bass.ds((NHP * i + hp) * P, P), :]).then_inc(k_in[hp % 2], 16)

            def load_v(i, n):
                sp.wait_ge(v_used, V_PIECES * i + n + 1)
                slot = n % V_SLOTS
                sp.dma_start(v_buf[:, slot * 1024:(slot + 1) * 1024],
                             d["v_used"][bass.ds((V_PIECES * i + n) * P, P), :]).then_inc(v_in[slot], 16)

            def load_round_start(i):
                t0 = QKV_TILES + ROUND_TILES * i
                load_w(t0, 0, t0)
                load_w(t0 + 1, 1, t0)
                load_k(i, 0)
                load_k(i, 1)
                for n in range(V_SLOTS):
                    load_v(i, n)

            def load_round_rest(i):
                t0 = QKV_TILES + ROUND_TILES * i
                load_w(t0 + 2, 0, t0 + 1)
                load_k(i, 2)
                load_w(t0 + 3, 1, t0 + 2)
                load_k(i, 3)
                load_w(t0 + 4, 0, t0 + 3)

            load_w(0, 0, None)
            for n, (k0, k1) in enumerate(X_CHUNKS):
                c = slice(k0 * NT, k1 * NT)
                sp.dma_start(x_raw[:, c], d["xT"][:, c]).then_inc(x_in[n], 16)
            load_w(1, 1, None)
            for tensor, name in ((ident, "ident"), (mask_pr, "mask_pr"), (mask_new, "mask_new"), (state, "state"),
                                 (conv_w, "conv_w")):
                sp.dma_start(tensor[:, :], d[name]).then_inc(small_in, 16)
            sp.dma_start(mask_s[:, 0:USED], d["mask_s"]).then_inc(small_in, 16)
            between = {3: [(load_k, 0)], 5: [(load_k, 1)], 7: [(load_v, 0), (load_v, 1)],
                       9: [(load_v, 2), (load_v, 3)], 11: [(load_v, 4)]}
            for tile in range(2, QKV_TILES):
                load_w(tile, tile % 2, tile - 1)
                if tile == 3:
                    sp.wait_ge(x_lo_done, len(X_CHUNKS))
                for load, n in between.get(tile, ()):
                    load(0, n)
            load_w(QKV_TILES, 0, QKV_TILES - 1)
            load_w(QKV_TILES + 1, 1, QKV_TILES)
            sp.wait_ge(qkv_a_read, 2 * NHP)
            sp.wait_ge(qkv_b_read, 2 * NHP)
            sp.dma_start(d["kT_new"], qk[:, NHP * NT:]).then_inc(kv_out, 16)
            sp.wait_ge(vt_read, NHP)
            sp.dma_start(d["v_prompt"].rearrange("(t p) n -> p t n", p=P),
                         v_rows[:, :].rearrange("p (t n) -> p t n", t=QT)).then_inc(kv_out, 16)
            sp.wait_ge(vn_read, NHP)
            sp.dma_start(d["v_sample"], v_new[:, :]).then_inc(kv_out, 16)

            with sp.Fori(0, NPAIR - 1) as i:
                load_round_rest(i)
                for n in range(V_SLOTS, V_PIECES):
                    load_v(i, n)
                load_round_start(i + 1)
            load_round_rest(NPAIR - 1)
            sp.wait_ge(kv_out, 48)
            sp.wait_ge(k_used, 2 + NHP * NPAIR)
            sp.wait_ge(pr_pv, 1 + UNITS * NPAIR)
            sp.wait_ge(s_masked, 1 + 3 * NPAIR)
            v_before = {3: (5, 6), 4: (7,), 5: (8,), 6: (9,)}
            for n in range(KT):
                for v in v_before.get(n, ()):
                    load_v(NPAIR - 1, v)
                sp.dma_start(wo_raw[:, n * 2048 + 1024:(n + 1) * 2048],
                             d["w_out"][n * P:(n + 1) * P, :]).then_inc(wo_in[n], 16)
            sp.wait_ge(s_pv, 1 + NPAIR)
            sp.dma_start(y_t[0:1, :], d["ln_gb"]).then_inc(ln_in, 16)
            sp.wait_ge(new_conv_done, 1 + 2 * NPAIR)
            sp.dma_start(d["new_conv"], new_conv[:, :]).then_inc(conv_out, 16)
            for t in range(QT + 1):
                rows = P if t < QT else NS
                if t >= 2:
                    sp.wait_ge(r_done, 2 * (t - 1))
                sp.dma_start(x_res[0:rows, t % 2 * 1024:(t % 2 + 1) * 1024],
                             d["x_rows"][t * P:t * P + rows, :]).then_inc(res_in[t % 2], 16)
                if t >= 1:
                    sp.wait_ge(ln_done, t)
                    sp.dma_start(d["y"][(t - 1) * P:t * P, :],
                                 y_t[:, (t - 1) % 2 * 1024:((t - 1) % 2 + 1) * 1024]).then_inc(y_out[(t - 1) % 2], 16)
            sp.wait_ge(ln_done, QT + 1)
            sp.dma_start(d["y"][SEQ:NT, :], y_t[0:NS, QT % 2 * 1024:(QT % 2 + 1) * 1024]).then_inc(y_out[QT % 2], 16)
            sp.wait_ge(y_out[0], 16 * 3)
            sp.wait_ge(y_out[1], 16 * 2)
            sp.wait_ge(conv_out, 16)
            sp.wait_ge(copied, 16 * (2 * REST_ROWS + NPAIR * (NHP + V_PIECES // 2)))

        @block.gpsimd
        def _(pool):
            for opened in (new_conv_done,):
                pool.sem_inc(opened, 1)
            pool.memset(q_bd[:, :], 0.0).then_inc(zeroed, 1)
            pool.memset(u_pad[:, 0:2], 0.0).then_inc(zeroed, 1)
            pool.wait_ge(zeroed, 2)
            pool.wait_ge(small_in, 96)
            pool.wait_ge(qkv_a_read, 2 * NHP)
            pool.wait_ge(qkv_b_read, 2 * NHP)
            with pool.Fori(0, NPAIR) as i:
                pool.wait_ge(k_used, 2 + NHP * i)
                for e in range(2):
                    src = qk[e * 64:e * 64 + 64, 0:NHP * NT].rearrange("p (h t) -> p h t", t=NT)[
                        :, :, bass.ds(SEQ + 16 * i, 16)].rearrange("p h (b q) -> p h b q", b=2)
                    pool.tensor_copy(qbd_copy_ap(e), src).then_inc(qbd_done, 1)
                    pool.wait_ge(qbd_done, 2 * i + e + 1)
                pool.wait_ge(pr_pv, 1 + UNITS * i)
                pool.tensor_copy(q_st[:, :], qk[:, bass.ds(i * NT, SEQ)]).then_inc(staged, 1)
                pool.tensor_copy(k_st[:, :], qk[:, bass.ds((NHP + i) * NT, SEQ)]).then_inc(staged, 1)
                pool.wait_ge(vt_read, NHP)
                pool.tensor_copy(v_st[:, :].rearrange("p (t n) -> p t n", t=QT),
                                 v_rows[:, :].rearrange("p (t n) -> p t n", t=QT)[:, :, bass.ds(i * P, P)])\
                    .then_inc(v_staged, 1)
                pool.wait_ge(s_masked, 1 + 3 * i)
                pool.tensor_copy(mask_s[:, USED:], mask_new[:, bass.ds(i * NS, NS)]).then_inc(masked_new, 1)
                pool.wait_ge(v_staged, i + 1)
                pool.wait_ge(y_done, 1 + i)
                pool.wait_ge(new_conv_done, 1 + 2 * i)
                pool.tensor_copy(cw[:, :], conv_w[:, bass.ds(i * CONV_WIDTH, CONV_WIDTH)]).then_inc(padded, 1)
                pool.tensor_copy(u_s[:, :, 0:2],
                                 state[:, bass.ds(i * 2 * DEC_BATCH, 2 * DEC_BATCH)].rearrange("p (b t) -> p b t", t=2))\
                    .then_inc(padded, 1)
                pool.wait_ge(u_done, 1 + 3 * i + 3)
                pool.tensor_copy(new_conv[:, bass.ds(i * 18, 2)], u_pad[:, SEQ:SEQ + 2]).then_inc(new_conv_done, 1)
                pool.tensor_copy(new_conv[:, bass.ds(i * 18 + 2, 16)].rearrange("p (b t) -> p b t", t=2),
                                 u_s[:, :, DEC_SEQ:DEC_SEQ + 2]).then_inc(new_conv_done, 1)
            pool.wait_ge(ln_in, 16)
            pool.partition_broadcast(ln_g[:, :], y_t[0:1, 0:D_MODEL]).then_inc(ln_spread, 1)
            pool.partition_broadcast(ln_b[:, :], y_t[0:1, D_MODEL:]).then_inc(ln_spread, 1)

        @block.scalar
        def _(act):
            for opened in (s_out, so_moved):
                act.sem_inc(opened, 1)

            def split_hi(slot, loaded, used_before):
                act.wait_ge(w_in[slot], 16 * loaded)
                if used_before is not None:
                    act.wait_ge(pj_b_done, used_before)
                c = slice(slot * 1024, (slot + 1) * 1024)
                nc.scalar.copy(w_hi[:, c], w_raw[:, c]).then_inc(w_hi_done, 1)

            split_hi(0, 1, None)
            for n, (k0, k1) in enumerate(X_CHUNKS):
                c = slice(k0 * NT, k1 * NT)
                act.wait_ge(x_in[n], 16)
                nc.scalar.copy(x_hi[:, c], x_raw[:, c]).then_inc(x_hi_done, 1)
            split_hi(1, 1, None)

            def copy_rest_of(name, row):
                act.dma_start(d[name + "_out"][bass.ds(row * 256, 256), :],
                              d[name][bass.ds(row * 256, 256), :]).then_inc(copied, 16)

            def copy_rest(row):
                copy_rest_of("k_rest", row)
                copy_rest_of("v_rest", row)

            def copy_k(i, hp):
                rows = bass.ds((NHP * i + hp) * P, P)
                act.dma_start(d["k_used_out"][rows, :], d["k_used"][rows, :]).then_inc(copied, 16)

            def copy_v(i, s):
                rows = bass.ds((V_PIECES * i + 2 * s) * P, 2 * P)
                act.dma_start(d["v_used_out"][rows, :], d["v_used"][rows, :]).then_inc(copied, 16)

            copy_rest(0)
            with act.Fori(0, NHP) as m:
                for j in range(2):
                    act.wait_ge(pj_a_done, 2 * m + j + 1)
                    nc.scalar.copy(qk[:, bass.ds((2 * m + j) * NT, HALF)], pj_a[:, 0:HALF]).then_inc(qkv_a_read, 1)
                    split_hi(j, m + 2, 2 * m + j + 1)
                copy_rest(m + 1)
            for f in range(NHP):
                t = 2 * NHP + f
                act.wait_ge(pj_a_done, t + 1)
                if f >= 2:
                    act.wait_ge(vt_done, f - 1)
                nc.scalar.copy(v_stage[f % 2][:, 0:HALF], pj_a[:, 0:HALF]).then_inc(qkv_a_read, 1)
                if f < 2:
                    split_hi(f, NHP + 2, t + 1)
                if f == 0:
                    copy_rest(NHP + 1)
                elif f >= 2:
                    copy_rest_of(("k_rest", "v_rest")[f % 2], NHP + 2)
                if f >= 1:
                    act.wait_ge(vt_done, f)
                    nc.scalar.copy(v_rows[:, :].rearrange("p (t n) -> p t n", t=QT)[:, :, (f - 1) * P:f * P],
                                   pt[:, :].rearrange("p (t n) -> p t n", t=QT)).then_inc(vt_read, 1)
            act.wait_ge(vt_done, NHP)
            nc.scalar.copy(v_rows[:, :].rearrange("p (t n) -> p t n", t=QT)[:, :, (NHP - 1) * P:],
                           pt[:, :].rearrange("p (t n) -> p t n", t=QT)).then_inc(vt_read, 1)

            def exp_prompt(i, u):
                w = (UNIT_ORDER[u][1] + 1) * P
                act.wait_ge(pr_masked, 1 + UNITS * i + u + 1)
                p = p_pr[:, u % 2 * 512:u % 2 * 512 + w]
                nc.scalar.activation(p, p, ACT.Exp, bias=negmax_pr[:, u % 2:u % 2 + 1], scale=-1.0,
                                     accum_out=sum_pr[:, u % 2:u % 2 + 1]).then_inc(pr_exp, 1)

            def move_prompt(i, u):
                w = (UNIT_ORDER[u][1] + 1) * P
                act.wait_ge(pr_turned, 1 + UNITS * i + u + 1)
                act.wait_ge(pr_pv, 1 + UNITS * i + max(0, u - 1))
                nc.scalar.copy(pt_pr[:, u % 2 * 512:u % 2 * 512 + w], pt[:, 0:w]).then_inc(pr_moved, 1)

            def exp_gate(i, tile, bank_, done, c0):
                act.wait_ge(done, QKV_TILES + ROUND_TILES * i + tile + 1)
                act.wait_ge(mixed, 1 + 4 * i + (0 if tile == 3 else 1 + c0 // HALF))
                nc.scalar.activation(rg[:, c0:c0 + HALF], bank_[:, 0:HALF], ACT.Exp, scale=-1.0).then_inc(g_exp, 1)

            def split_wo(n):
                act.wait_ge(wo_in[n], 16)
                nc.scalar.copy(wo[:, n * 2048:n * 2048 + 1024], wo_raw[:, n * 2048 + 1024:(n + 1) * 2048])\
                    .then_inc(wo_hi_done, 1)

            def split_mix(n):
                need, k0, k1, c0, c1 = MIX_SPLITS[n]
                act.wait_ge(pj_b_done, W_TILES)
                act.wait_ge(mixed, 1 + need)
                nc.scalar.copy(token_cols(x_hi, k0, k1, c0, c1), token_cols(mix, k0, k1, c0, c1)).then_inc(m_hi_done, 1)

            def act_round(i, last=False):
                t0 = QKV_TILES + ROUND_TILES * i
                in0 = QKV_TILES // 2 + 3 * i
                in1 = QKV_TILES // 2 + 2 * i
                split_hi(0, in0 + 1, t0)
                for u in range(UNITS):
                    exp_prompt(i, u)
                    if u == 0:
                        split_hi(1, in1 + 1, t0)
                    if u in (1, 3):
                        h = u // 2
                        act.wait_ge((pj_a_done, pj_b_done)[h], t0 + 1)
                        act.wait_ge(u_done, 1 + 3 * i)
                        nc.scalar.copy(gcs[:, h * HALF:(h + 1) * HALF], (pj_a, pj_b)[h][:, 0:HALF])\
                            .then_inc(c_read[h], 1)
                    move_prompt(i, u)
                    if u == 4:
                        split_hi(0, in0 + 2, t0 + 1)
                    if u % 2 == 1:
                        copy_k(i, u // 2)
                    elif not last or u < 6:
                        copy_v(i, u // 2)
                act.wait_ge(s_max, i + 1)
                nc.scalar.activation(p_s[:, :], p_s[:, :], ACT.Exp, bias=negmax_s, scale=-1.0,
                                     accum_out=sum_s).then_inc(s_exp, 1)
                split_hi(1, in1 + 2, t0 + 2)
                act.wait_ge(pr_pv, 1 + UNITS * (i + 1))
                act.wait_ge(mixed, 1 + 4 * i)
                nc.scalar.copy(o_pr[:, :], po[:, :]).then_inc(pr_out, 1)
                split_hi(0, in0 + 3, t0 + 3)
                act.wait_ge(s_turned, 1 + 3 * i + 1)
                act.wait_ge(s_pv, 1 + i)
                nc.scalar.copy(pt_s[:, 0:512], pt[:, :]).then_inc(s_moved, 1)
                if last:
                    split_wo(0)
                exp_gate(i, 3, pj_a, pj_a_done, 0)
                act.wait_ge(s_turned, 1 + 3 * i + 2)
                nc.scalar.copy(pt_s[:, 512:1024], pt[:, :]).then_inc(s_moved, 1)
                if last:
                    split_wo(1)
                    split_wo(2)
                exp_gate(i, 3, pj_b, pj_b_done, HALF)
                act.wait_ge(s_turned, 1 + 3 * i + 3)
                nc.scalar.copy(pt_s[:, 1024:1280], pt[:, 0:256]).then_inc(s_moved, 1)
                nc.scalar.copy(pt_s[0:NS, 1280:1408], pt[0:NS, 256:384]).then_inc(s_moved, 1)
                if last:
                    split_wo(3)
                    split_wo(4)
                    copy_v(i, 3)
                    copy_v(i, 4)
                exp_gate(i, 4, pj_a, pj_a_done, 0)
                if last:
                    split_wo(5)
                exp_gate(i, 4, pj_b, pj_b_done, HALF)
                if last:
                    split_mix(0)
                    split_wo(6)
                act.wait_ge(s_pv, 1 + i + 1)
                act.wait_ge(so_turned, 1 + i)
                nc.scalar.copy(o_s[:, :], po[:, :]).then_inc(s_out, 1)
                if last:
                    split_wo(7)
                act.wait_ge(so_turned, 1 + i + 1)
                for e in range(2):
                    dst = att_s[e * 64:e * 64 + 64, :].rearrange("p (h t) -> p h t", t=NS)[
                        :, :, bass.ds(16 * i, 16)].rearrange("p h (b q) -> p h b q", b=2)
                    nc.scalar.copy(dst, diagonal_ap(e)).then_inc(so_moved, 1)

            with act.Fori(0, NPAIR - 1) as i:
                act_round(i)
            act_round(NPAIR - 1, last=True)

            def copy_late(n):
                if n < NPAIR - 1:
                    copy_v(n, 4)
                elif n < LATE_COPIES:
                    n -= NPAIR - 1
                    copy_rest_of(("k_rest", "v_rest")[n % 2], NHP + 3 + n // 2)

            for n in range(1, len(MIX_SPLITS)):
                split_mix(n)
                copy_late(n - 1)
            copy_late(5)
            for t in range(QT + 1):
                rows = P if t < QT else NS
                act.wait_ge(ln_step, 5 * t + 4)
                nc.scalar.activation(std[0:rows, :], rstd[0:rows, :], ACT.Sqrt).then_inc(ln_sqrt, 1)
                for n in range(6 + 2 * t, 8 + 2 * t):
                    copy_late(n)

        @block.vector
        def _(dve):
            for opened in (pr_masked, s_masked, mixed, u_done, y_done):
                dve.sem_inc(opened, 1)

            def split_lo(slot, n):
                dve.wait_ge(w_hi_done, n)
                c = slice(slot * 1024, (slot + 1) * 1024)
                nc.vector.tensor_tensor(w_lo[:, c], w_raw[:, c], w_hi[:, c].bitcast(F32), ALU.subtract)\
                    .then_inc(w_lo_done, 1)

            split_lo(0, 1)
            for n, (k0, k1) in enumerate(X_CHUNKS):
                c = slice(k0 * NT, k1 * NT)
                dve.wait_ge(x_hi_done, n + 1)
                nc.vector.tensor_tensor(x_lo[:, c], x_raw[:, c], x_hi[:, c].bitcast(F32), ALU.subtract)\
                    .then_inc(x_lo_done, 1)
            split_lo(1, 2)

            with dve.Fori(0, NHP) as m:
                for j in range(2):
                    dve.wait_ge(pj_b_done, 2 * m + j + 1)
                    nc.vector.tensor_copy(qk[:, bass.ds((2 * m + j) * NT + HALF, HALF)], pj_b[:, 0:HALF])\
                        .then_inc(qkv_b_read, 1)
                    split_lo(j, 2 * m + j + 3)
            for f in range(NHP):
                t = 2 * NHP + f
                dve.wait_ge(pj_b_done, t + 1)
                if f >= 2:
                    dve.wait_ge(vt_done, f - 1)
                nc.vector.tensor_copy(v_stage[f % 2][:, HALF:], pj_b[:, 0:HALF]).then_inc(qkv_b_read, 1)
                if f < 2:
                    split_lo(f, t + 3)
                if f >= 1:
                    dve.wait_ge(vt_done, f)
                    nc.vector.tensor_copy(v_new[:, (f - 1) * P:f * P], po[0:NS, 0:P]).then_inc(vn_read, 1)
            dve.wait_ge(vt_done, NHP)
            nc.vector.tensor_copy(v_new[:, (NHP - 1) * P:], po[0:NS, 0:P]).then_inc(vn_read, 1)
            dve.wait_ge(small_in, 96)

            def mask_prompt(i, u):
                t = UNIT_ORDER[u][1]
                w = (t + 1) * P
                dve.wait_ge(small_in, 96)
                dve.wait_ge(pr_turned, 1 + UNITS * i + max(0, u - 1))
                dve.wait_ge(pr_scores, UNITS * i + u + 1)
                dve.sem_inc(may_mask, 1)
                nc.vector.tensor_tensor_reduce(
                    out=p_pr[:, u % 2 * 512:u % 2 * 512 + w], in0=px[:, 0:w], in1=mask_pr[:, SEQ - w:],
                    scale=-SCALE, scalar=BIG, op0=ALU.add, op1=ALU.min,
                    accum_out=negmax_pr[:, u % 2:u % 2 + 1]).then_inc(pr_masked, 1)

            def norm_prompt(i, u):
                w = (UNIT_ORDER[u][1] + 1) * P
                s = slice(u % 2, u % 2 + 1)
                dve.wait_ge(pr_exp, UNITS * i + u + 1)
                nc.vector.reciprocal(inv_pr[:, s], sum_pr[:, s]).then_inc(pr_inv, 1)
                dve.wait_ge(pr_inv, UNITS * i + u + 1)
                p = p_pr[:, u % 2 * 512:u % 2 * 512 + w]
                nc.vector.tensor_scalar(p, p, inv_pr[:, s], None, ALU.mult).then_inc(pr_norm, 1)

            def gate_half(i, tile, bank_, h):
                c = slice(h * HALF, (h + 1) * HALF)
                n = 2 * (tile - 3) + h
                dve.wait_ge(g_exp, 4 * i + n + 1)
                step = 12 * i + 3 * n
                nc.vector.tensor_scalar(rg[:, c], rg[:, c], 1.0, None, ALU.add).then_inc(g_step, 1)
                dve.wait_ge(g_step, step + 1)
                nc.vector.reciprocal(rg[:, c], rg[:, c]).then_inc(g_step, 1)
                dve.wait_ge(g_step, step + 2)
                if tile == 3:
                    nc.vector.tensor_tensor(rg[:, c], rg[:, c], zb[:, c], ALU.mult).then_inc(g_step, 1)
                else:
                    if h == 0:
                        dve.wait_ge(pr_out, i + 1)
                    e = slice(h * HALF, min((h + 1) * HALF, SEQ))
                    nc.vector.tensor_tensor(rg[:, e], rg[:, e], o_pr[:, e], ALU.mult).then_inc(g_step, 1)
                dve.wait_ge(g_step, step + 3)
                row = (NHP if tile == 3 else 0) + i
                nc.vector.tensor_tensor(mix[:, bass.ds(row * NT + h * HALF, HALF)], bank_[:, 0:HALF], rg[:, c],
                                        ALU.mult).then_inc(mixed, 1)

            def split_wo_lo(n):
                dve.wait_ge(wo_hi_done, n + 1)
                lo = slice(n * 2048 + 1024, (n + 1) * 2048)
                nc.vector.tensor_tensor(wo[:, lo], wo_raw[:, lo], wo[:, n * 2048:n * 2048 + 1024].bitcast(F32),
                                        ALU.subtract).then_inc(wo_lo_done, 1)

            def split_mix_lo(n):
                _, k0, k1, c0, c1 = MIX_SPLITS[n]
                dve.wait_ge(m_hi_done, n + 1)
                nc.vector.tensor_tensor(token_cols(x_lo, k0, k1, c0, c1), token_cols(mix, k0, k1, c0, c1),
                                        token_cols(x_hi, k0, k1, c0, c1).bitcast(F32), ALU.subtract)\
                    .then_inc(m_lo_done, 1)

            def dve_round(i, last=False):
                t0 = QKV_TILES + ROUND_TILES * i
                for u in range(UNITS):
                    mask_prompt(i, u)
                    if u == 0:
                        split_lo(0, t0 + 1)
                    norm_prompt(i, u)
                    if u == 0:
                        split_lo(1, t0 + 2)
                    if u == 4:
                        split_lo(0, t0 + 3)
                    if u == 5:
                        dve.wait_ge(pj_a_done, t0 + 2)
                        dve.wait_ge(padded, 2 * i + 2)
                        dve.wait_ge(c_read[0], i + 1)
                        nc.vector.tensor_tensor(u_pad[:, 2:2 + HALF], pj_a[:, 0:HALF], gcs[:, 0:HALF], ALU.mult)\
                            .then_inc(u_done, 1)
                dve.wait_ge(small_in, 96)
                dve.wait_ge(k_used, 2 + NHP * i + NHP)
                dve.wait_ge(masked_new, i + 1)
                dve.wait_ge(s_turned, 1 + 3 * i)
                dve.sem_inc(may_mask, 1)
                for c, (c0, w) in enumerate(CHUNKS):
                    w = w + (NS if c == 2 else 0)
                    nc.vector.tensor_tensor_reduce(
                        out=p_s[:, c0:c0 + w], in0=sc[c][:, 0:w], in1=mask_s[:, c0:c0 + w],
                        scale=-SCALE, scalar=BIG, op0=ALU.add, op1=ALU.min,
                        accum_out=negmax3[:, c:c + 1]).then_inc(s_masked, 1)
                dve.wait_ge(s_masked, 1 + 3 * i + 3)
                nc.vector.tensor_reduce(negmax_s, negmax3, AX_X, ALU.min).then_inc(s_max, 1)
                dve.wait_ge(pj_b_done, t0 + 2)
                dve.wait_ge(c_read[1], i + 1)
                nc.vector.tensor_tensor(u_pad[:, 2 + HALF:2 + SEQ], pj_b[:, 0:HP_LEFT], gcs[:, HALF:SEQ], ALU.mult)\
                    .then_inc(u_done, 1)
                nc.vector.tensor_tensor(u_s[:, :, 2:], pj_b[:, HP_LEFT:HALF].rearrange("p (b t) -> p b t", t=DEC_SEQ),
                                        gcs[:, SEQ:].rearrange("p (b t) -> p b t", t=DEC_SEQ), ALU.mult)\
                    .then_inc(u_done, 1)
                n = PAD_COLS - 2
                dve.wait_ge(u_done, 1 + 3 * i + 3)
                nc.vector.tensor_scalar(y_pad[:, 0:n], u_pad[:, 0:n], cw[:, 0:1], None, ALU.mult).then_inc(y_step, 1)
                dve.wait_ge(s_exp, i + 1)
                nc.vector.reciprocal(inv_s, sum_s).then_inc(s_inv, 1)
                dve.wait_ge(s_inv, i + 1)
                nc.vector.tensor_scalar(p_s[:, :], p_s[:, :], inv_s, None, ALU.mult).then_inc(s_norm, 1)
                dve.wait_ge(y_step, 2 * i + 1)
                nc.vector.scalar_tensor_tensor(y_pad[:, 0:n], u_pad[:, 1:n + 1], cw[:, 1:2], y_pad[:, 0:n],
                                               ALU.mult, ALU.add).then_inc(y_step, 1)
                split_lo(1, t0 + 4)
                dve.wait_ge(y_step, 2 * i + 2)
                nc.vector.scalar_tensor_tensor(y_pad[:, 0:n], u_pad[:, 2:n + 2], cw[:, 2:3], y_pad[:, 0:n],
                                               ALU.mult, ALU.add).then_inc(y_done, 1)
                dve.wait_ge(y_done, 1 + i + 1)
                dve.wait_ge(pj_a_done, t0 + 3)
                nc.vector.tensor_tensor(zb[:, 0:HALF], pj_a[:, 0:HALF], y_pad[:, 0:HALF], ALU.mult).then_inc(z_done, 1)
                dve.wait_ge(pj_b_done, t0 + 3)
                nc.vector.tensor_tensor(zb[:, HALF:SEQ], pj_b[:, 0:HP_LEFT], y_pad[:, HALF:SEQ], ALU.mult)\
                    .then_inc(z_done, 1)
                nc.vector.tensor_tensor(zb[:, SEQ:].rearrange("p (b t) -> p b t", t=DEC_SEQ),
                                        pj_b[:, HP_LEFT:HALF].rearrange("p (b t) -> p b t", t=DEC_SEQ),
                                        y_s[:, :, 0:DEC_SEQ], ALU.mult).then_inc(z_done, 1)
                split_lo(0, t0 + 5)
                if last:
                    split_wo_lo(0)
                dve.wait_ge(z_done, 3 * i + 3)
                gate_half(i, 3, pj_a, 0)
                if last:
                    split_wo_lo(1)
                    split_wo_lo(2)
                gate_half(i, 3, pj_b, 1)
                if last:
                    split_wo_lo(3)
                    split_wo_lo(4)
                gate_half(i, 4, pj_a, 0)
                if last:
                    split_wo_lo(5)
                    split_mix_lo(0)
                gate_half(i, 4, pj_b, 1)
                if last:
                    split_mix_lo(1)
                    split_wo_lo(6)
                    split_wo_lo(7)

            with dve.Fori(0, NPAIR - 1) as i:
                dve_round(i)
            dve_round(NPAIR - 1, last=True)

            for n in range(2, len(MIX_SPLITS)):
                if n == len(MIX_SPLITS) - 1:
                    dve.wait_ge(so_moved, 1 + 2 * NPAIR)
                    dve.wait_ge(mixed, 1 + 4 * NPAIR)
                    m = token_cols(mix, 0, NHP, SEQ, NT)
                    nc.vector.tensor_tensor(m, m, att_s[:, :].rearrange("p (h t) -> p h t", t=NS), ALU.mult)\
                        .then_inc(mixed, 1)
                split_mix_lo(n)

            dve.wait_ge(ln_spread, 2)
            for t in range(QT + 1):
                rows = P if t < QT else NS
                banks = (sc[0], sc[1]) if t % 2 == 0 else (sc[2], px)
                y = y_t[0:rows, t % 2 * 1024:(t % 2 + 1) * 1024]
                xr = x_res[0:rows, t % 2 * 1024:(t % 2 + 1) * 1024]
                step = 5 * t
                dve.wait_ge(res_in[t % 2], 16 * (t // 2 + 1))
                if t >= 2:
                    dve.wait_ge(y_out[t % 2], 16 * (t // 2))
                for h in range(2):
                    c = slice(h * 512, (h + 1) * 512)
                    dve.wait_ge(o_done, 2 * t + h + 1)
                    nc.vector.scalar_tensor_tensor(y[:, c], xr[:, c], ALPHA, banks[h][0:rows, :], ALU.mult, ALU.add)\
                        .then_inc(r_done, 1)
                for h in range(2):
                    dve.wait_ge(r_done, 2 * t + h + 1)
                    nc.vector.bn_stats(bn[0:rows, 6 * h:6 * h + 6], y[:, h * 512:(h + 1) * 512]).then_inc(ln_step, 1)
                dve.wait_ge(ln_step, step + 2)
                nc.vector.bn_aggr(mv[0:rows, :], bn[0:rows, :]).then_inc(ln_step, 1)
                dve.wait_ge(ln_step, step + 3)
                nc.vector.tensor_scalar(rstd[0:rows, :], mv[0:rows, 1:2], LN_EPS, None, ALU.add).then_inc(ln_step, 1)
                nc.vector.scalar_tensor_tensor(y, y, mv[0:rows, 0:1], ln_g[0:rows, :], ALU.subtract, ALU.mult)\
                    .then_inc(ln_scaled, 1)
                dve.wait_ge(ln_sqrt, t + 1)
                nc.vector.reciprocal(rstd[0:rows, :], std[0:rows, :]).then_inc(ln_step, 1)
                dve.wait_ge(ln_step, step + 5)
                dve.wait_ge(ln_scaled, t + 1)
                nc.vector.scalar_tensor_tensor(y, y, rstd[0:rows, :], ln_b[0:rows, :], ALU.mult, ALU.add)\
                    .then_inc(ln_done, 1)

        @block.tensor
        def _(pe):
            def product(slot, k, h):
                out = (pj_a, pj_b)[h][:, 0:HALF]
                w = slice(slot * 1024 + k * P, slot * 1024 + (k + 1) * P)
                c = slice(k * NT + h * HALF, k * NT + (h + 1) * HALF)
                nc.tensor.matmul(out, w_hi[:, w], x_hi[:, c], start=(k == 0), stop=False)
                nc.tensor.matmul(out, w_hi[:, w], x_lo[:, c], start=False, stop=False)
                return nc.tensor.matmul(out, w_lo[:, w], x_hi[:, c], start=False, stop=(k == KT - 1))

            def project(slot, tile, h, *reads):
                if h == 0:
                    pe.wait_ge(w_lo_done, tile + 1)
                for read, count in reads:
                    pe.wait_ge(read, count)
                for k in range(KT):
                    last = product(slot, k, h)
                last.then_inc((pj_a_done, pj_b_done)[h], 1)

            def turn_v(f):
                pe.wait_ge(qkv_a_read, 2 * NHP + f + 1)
                pe.wait_ge(qkv_b_read, 2 * NHP + f + 1)
                if f == 0:
                    pe.wait_ge(small_in, 96)
                else:
                    pe.wait_ge(vt_read, f)
                    pe.wait_ge(vn_read, f)
                v = v_stage[f % 2]
                for t in range(QT):
                    nc.tensor.transpose(pt[:, t * P:(t + 1) * P], v[:, t * P:(t + 1) * P], ident[:, :])
                nc.tensor.transpose(po[0:NS, 0:P], v[:, SEQ:], ident[:, :]).then_inc(vt_done, 1)

            for opened in (pr_turned, pr_pv, s_turned, s_pv, so_turned):
                pe.sem_inc(opened, 1)
            pe.sem_inc(k_used, 2)
            pe.sem_inc(v_used, V_SLOTS)
            pe.wait_ge(w_lo_done, 1)
            for n, (k0, k1) in enumerate(X_CHUNKS):
                pe.wait_ge(x_lo_done, n + 1)
                for k in range(k0, k1):
                    last = [product(0, k, h) for h in range(2)]
            for h in range(2):
                last[h].then_inc((pj_a_done, pj_b_done)[h], 1)
            qkv_read = (qkv_a_read, qkv_b_read)
            project(1, 1, 0, (qkv_read[0], 1))
            project(1, 1, 1, (qkv_read[1], 1))
            with pe.Fori(1, NHP) as m:
                for j in range(2):
                    for h in range(2):
                        project(j, 2 * m + j, h, (qkv_read[h], 2 * m + j))
            for f in range(NHP):
                for h in range(2):
                    project(f % 2, 2 * NHP + f, h, (qkv_read[h], 2 * NHP + f))
                if f >= 1:
                    turn_v(f - 1)
            turn_v(NHP - 1)

            def prompt_scores(i, u):
                e, t = UNIT_ORDER[u]
                if u == 0:
                    pe.wait_ge(staged, 2 * i + 2)
                pe.wait_ge(pr_masked, 1 + UNITS * i + u)
                w = (t + 1) * P
                nc.tensor.matmul(px[:, 0:w], q_st[e * 64:e * 64 + 64, t * P:(t + 1) * P],
                                 k_st[e * 64:e * 64 + 64, 0:w], start=True, stop=True).then_inc(pr_scores, 1)

            def prompt_turn(i, u):
                t = UNIT_ORDER[u][1]
                pe.wait_ge(pr_norm, UNITS * i + u + 1)
                if u == 0:
                    pe.wait_ge(so_moved, 1 + 2 * i)
                    pe.wait_ge(vt_read, NHP)
                else:
                    pe.wait_ge(pr_moved, UNITS * i + u)
                for k in range(t + 1):
                    c = u % 2 * 512 + k * P
                    last = nc.tensor.transpose(pt[:, k * P:(k + 1) * P], p_pr[:, c:c + P], ident[:, :])
                last.then_inc(pr_turned, 1)

            def prompt_values(i, u):
                e, t = UNIT_ORDER[u]
                pe.wait_ge(pr_moved, UNITS * i + u + 1)
                if u == 0:
                    pe.wait_ge(s_out, 1 + i)
                    pe.wait_ge(vn_read, NHP)
                    pe.wait_ge(v_staged, i + 1)
                for k in range(t + 1):
                    last = nc.tensor.matmul(po[e * 64:e * 64 + 64, t * P:(t + 1) * P],
                                            v_st[:, k * P + e * 64:k * P + e * 64 + 64],
                                            pt_pr[:, u % 2 * 512 + k * P:u % 2 * 512 + (k + 1) * P],
                                            start=(k == 0), stop=(k == t))
                last.then_inc(pr_pv, 1)

            def sample_scores(i, hp):
                pe.wait_ge(k_in[hp % 2], 16 * (2 * i + hp // 2 + 1))
                if hp == 0:
                    pe.wait_ge(qbd_done, 2 * i + 2)
                    pe.wait_ge(s_masked, 1 + 3 * i)
                for c, (c0, w) in enumerate(CHUNKS):
                    for b in range(2):
                        rows = slice(b * 64, b * 64 + 64)
                        q = q_bd[:, hp * P + b * 64:hp * P + b * 64 + 64]
                        k0 = hp % 2 * 2560 + b * USED + c0
                        last = nc.tensor.matmul(sc[c][rows, 0:w], q, k_buf[:, k0:k0 + w], start=(hp == 0),
                                                stop=(hp == NHP - 1 and c < 2), skip_group_check=True)
                        if c == 2:
                            last = nc.tensor.matmul(sc[c][rows, w:w + NS], q,
                                                    qk[:, (NHP + hp) * NT + SEQ:(NHP + hp + 1) * NT],
                                                    start=False, stop=(hp == NHP - 1), skip_group_check=True)
                last.then_inc(k_used, 1)

            def sample_turn(i, g):
                if g == 0:
                    pe.wait_ge(s_norm, i + 1)
                    pe.wait_ge(pr_moved, UNITS * (i + 1))
                else:
                    pe.wait_ge(s_moved, 4 * i + g)
                tiles = range(4 * g, min(4 * g + 4, USED_TILES))
                for n, t in enumerate(tiles):
                    last = nc.tensor.transpose(pt[:, n * P:(n + 1) * P], p_s[:, t * P:(t + 1) * P], ident[:, :])
                if g == 2:
                    last = nc.tensor.transpose(pt[0:NS, 256:384], p_s[:, USED:], ident[:, :])
                last.then_inc(s_turned, 1)

            def sample_values(i, s):
                pe.wait_ge(s_moved, 4 * i + (s // 2 + 1 if s < V_PIECES // 2 - 1 else 4))
                if s == 0:
                    pe.wait_ge(pr_out, i + 1)
                for b in range(2):
                    n = 2 * s + b
                    pe.wait_ge(v_in[n % V_SLOTS], 16 * (2 * i + n // V_SLOTS + 1))
                for half in range(2):
                    for b in range(2):
                        n = 2 * s + b
                        t = 2 * s + half
                        v0 = n % V_SLOTS * 1024 + half * 512
                        last = nc.tensor.matmul(po[b * 64:b * 64 + 64, :],
                                                pt_s[:, t * P + b * 64:t * P + b * 64 + 64],
                                                v_buf[:, v0:v0 + 512], start=(t == 0), stop=False)
                        if half == 1:
                            last.then_inc(v_used, 1)
                if s == V_PIECES // 2 - 1:
                    for b in range(2):
                        last = nc.tensor.matmul(po[b * 64:b * 64 + 64, :],
                                                pt_s[0:NS, USED + b * 64:USED + b * 64 + 64],
                                                v_new[:, :], start=False, stop=True)
                    last.then_inc(s_pv, 1)

            def sample_out_turn(i):
                pe.wait_ge(s_out, 1 + i + 1)
                for hp in range(NHP):
                    last = nc.tensor.transpose(pt[:, hp * P:(hp + 1) * P], o_s[:, hp * P:(hp + 1) * P], ident[:, :])
                last.then_inc(so_turned, 1)

            def pe_round(i):
                t0 = QKV_TILES + ROUND_TILES * i
                for u in range(UNITS):
                    prompt_scores(i, u)
                    h = u // 2 % 2
                    if u % 2 == 0:
                        sample_scores(i, u // 2)
                    elif u < NHP:
                        project(0, t0, h, (mixed, 1 + 4 * i), (qkv_read[h], QKV_TILES))
                    else:
                        project(1, t0 + 1, h, (c_read[h], i + 1))
                    prompt_turn(i, u)
                    if u:
                        prompt_values(i, u - 1)
                project(0, t0 + 2, 0, (u_done, 1 + 3 * i + 1))
                prompt_values(i, UNITS - 1)
                project(0, t0 + 2, 1, (u_done, 1 + 3 * i + 3))
                sample_turn(i, 0)
                project(1, t0 + 3, 0, (z_done, 3 * i + 1))
                sample_values(i, 0)
                sample_turn(i, 1)
                sample_values(i, 1)
                project(1, t0 + 3, 1, (z_done, 3 * i + 3))
                sample_values(i, 2)
                sample_turn(i, 2)
                project(0, t0 + 4, 0, (mixed, 1 + 4 * i + 1))
                sample_values(i, 3)
                project(0, t0 + 4, 1, (mixed, 1 + 4 * i + 2))
                sample_values(i, 4)
                sample_out_turn(i)

            with pe.Fori(0, NPAIR) as i:
                pe_round(i)

            pe.wait_ge(s_masked, 1 + 3 * NPAIR)
            pe.wait_ge(pr_masked, 1 + UNITS * NPAIR)
            for t in range(QT + 1):
                rows = P if t < QT else NS
                banks = (sc[0], sc[1]) if t % 2 == 0 else (sc[2], px)
                if t >= 2:
                    pe.wait_ge(r_done, 2 * (t - 1))
                parts = ((0, 0, NHP), (1, 0, NHP), (0, NHP, KT), (1, NHP, KT)) if t == 0 else ((0, 0, KT), (1, 0, KT))
                for part, (h, n0, n1) in enumerate(parts):
                    out = banks[h][0:rows, :]
                    if t == 0:
                        pe.wait_ge(m_lo_done, 1 + part // 2)
                    else:
                        pe.wait_ge(m_lo_done, t + 2)
                    for n in range(n0, n1):
                        k = MIX_ORDER[n]
                        if t == 0 and h == 0:
                            pe.wait_ge(wo_lo_done, n + 1)
                        tok = slice(k * NT + t * P, k * NT + t * P + rows)
                        hi = slice(n * 2048 + h * 512, n * 2048 + (h + 1) * 512)
                        lo = slice(n * 2048 + 1024 + h * 512, n * 2048 + 1024 + (h + 1) * 512)
                        nc.tensor.matmul(out, x_hi[:, tok], wo[:, hi], start=(n == 0), stop=False)
                        nc.tensor.matmul(out, x_hi[:, tok], wo[:, lo], start=False, stop=False)
                        last = nc.tensor.matmul(out, x_lo[:, tok], wo[:, hi], start=False, stop=(n == KT - 1))
                    if n1 == KT:
                        last.then_inc(o_done, 1)



def log_count(distance):
    d = np.asarray(distance)
    count = sum(((d >= 0) & (d <= w) & (d % r == 0)).astype(np.int64) for w, r in PAIRS)
    return np.where(count > 0, np.log(np.maximum(count, 1)), NEG)


def mask_arrays():
    p = np.arange(P)
    cached = np.empty((USED_TILES, P), np.int64)
    for r in range(8):
        cached[r] = 16 * p + r
    for s in range(2):
        cached[8 + s] = PAST_LEN - 512 + 16 * (p % 32) + 8 + 2 * (p // 32) + s
    row = np.arange(P)
    batch, query = row // 64, row % DEC_SEQ
    mask_s = log_count(PAST_LEN + query[:, None] - cached.reshape(1, -1))
    col = np.arange(NS)
    new = []
    for pair in range(NPAIR):
        m = log_count(query[:, None] - col[None, :] % DEC_SEQ)
        new.append(np.where(col[None, :] // DEC_SEQ == 2 * pair + batch[:, None], m, NEG))
    mask_pr = log_count(p[:, None] + SEQ - P - np.arange(SEQ)[None, :])
    scaled = [np.maximum(m / SCALE, NEG).astype(np.float32) for m in (mask_s, np.concatenate(new, 1), mask_pr)]
    return dict(zip(("mask_s", "mask_new", "mask_pr"), scaled))



def split_cache(c):
    c = np.asarray(c).reshape(DEC_BATCH, P, 16, D_ATT)
    old = c[:, :, 0:8].transpose(0, 2, 1, 3)
    recent = c[:, 96:, 8:].reshape(DEC_BATCH, 32, 4, 2, D_ATT).transpose(0, 3, 2, 1, 4)
    return np.concatenate([old, recent.reshape(DEC_BATCH, 2, P, D_ATT)], 1), c[:, :96, 8:]


def join_cache(used, rest, new):
    c = np.empty((DEC_BATCH, P, 16, D_ATT), np.float32)
    c[:, :, 0:8] = used[:, 0:8].transpose(0, 2, 1, 3)
    c[:, 96:, 8:] = used[:, 8:].reshape(DEC_BATCH, 2, 4, 32, D_ATT).transpose(0, 3, 2, 1, 4)\
        .reshape(DEC_BATCH, 32, 8, D_ATT)
    c[:, :96, 8:] = rest.reshape(DEC_BATCH, 96, 8, D_ATT)
    c = np.concatenate([c.reshape(DEC_BATCH, PAST_LEN, D_ATT)[:, DEC_SEQ:], new], 1)
    return c.reshape(DEC_BATCH, PAST_LEN, N_HEADS, HEAD_DIM)


def kernel(x_prompt, x_sample, cache_k, cache_v, state_conv, w_in, conv_w, w_out, ln_g, ln_b):
    import concourse.bacc as bacc
    from concourse.bass_utils import run_bass_kernel_spmd

    a = {}
    x = np.concatenate([np.asarray(x_prompt).reshape(SEQ, D_MODEL), np.asarray(x_sample).reshape(NS, D_MODEL)])
    a["x_rows"] = x
    a["xT"] = x.reshape(NT, KT, P).transpose(2, 1, 0).reshape(P, KT * NT)
    order = list(range(QKV_TILES)) + [NHP * g + i for i in range(NPAIR) for g in (5, 6, 4, 7, 3)]
    w = np.asarray(w_in).reshape(KT, P, 32, P).transpose(2, 1, 0, 3)[order].reshape(32 * P, 1024)
    wo = np.asarray(w_out).reshape(KT, P, D_MODEL)[list(MIX_ORDER)].reshape(KT * P, D_MODEL)
    a["w_tiles"], a["w_out"] = w, wo
    k_used, k_rest = split_cache(cache_k)
    v_used, v_rest = split_cache(cache_v)
    a["k_used"] = k_used.reshape(NPAIR, 2, USED, NHP, P).transpose(0, 3, 4, 1, 2).reshape(NPAIR * NHP * P, 2 * USED)
    a["v_used"] = v_used.reshape(NPAIR, 2, 5, 2, P, D_ATT).transpose(0, 2, 1, 4, 3, 5).reshape(NPAIR * 10 * P, 1024)
    a["k_rest"], a["v_rest"] = (r.reshape(REST_ROWS * 256, 1024) for r in (k_rest, v_rest))
    a["state"] = np.asarray(state_conv).reshape(DEC_BATCH, 2, NHP, P).transpose(3, 2, 0, 1).reshape(P, -1)
    a["conv_w"] = np.asarray(conv_w).reshape(CONV_WIDTH, NHP, P).transpose(2, 1, 0).reshape(P, -1)
    a["ln_gb"] = np.concatenate([np.asarray(ln_g), np.asarray(ln_b)]).reshape(1, -1)
    a["ident"] = np.eye(P, dtype=np.float32)
    a.update(mask_arrays())
    a = {name: np.ascontiguousarray(v) for name, v in a.items()}
    outs = {
        "y": (NT, D_MODEL), "kT_new": (P, NHP * NT), "v_prompt": (SEQ, D_ATT), "v_sample": (NS, D_ATT),
        "new_conv": (P, NHP * 18),
        **{name + "_out": a[name].shape for name in ("k_used", "v_used", "k_rest", "v_rest")},
    }
    nc = bacc.Bacc("TRN2", target_bir_lowering=False, num_devices=1)
    d = {n: nc.dram_tensor("in_" + n, v.shape, F32, kind="ExternalInput").ap() for n, v in a.items()}
    d.update({n: nc.dram_tensor("out_" + n, s, F32, kind="ExternalOutput").ap() for n, s in outs.items()})
    layer_step(nc, d)
    got = run_bass_kernel_spmd(nc, [{"in_" + n: v for n, v in a.items()}], core_ids=[0]).results[0]
    r = {n: got["out_" + n] for n in outs}

    y = r["y"]
    k_rows = r["kT_new"].reshape(P, NHP, NT).transpose(2, 1, 0).reshape(NT, D_ATT)
    k_used = r["k_used_out"].reshape(NPAIR, NHP, P, 2, USED_TILES, P).transpose(0, 3, 4, 5, 1, 2)\
        .reshape(DEC_BATCH, USED_TILES, P, D_ATT)
    v_used = r["v_used_out"].reshape(NPAIR, 5, 2, P, 2, D_ATT).transpose(0, 2, 1, 4, 3, 5)\
        .reshape(DEC_BATCH, USED_TILES, P, D_ATT)
    conv = r["new_conv"].reshape(P, NHP, 18).transpose(2, 1, 0).reshape(18, D_ATT)
    prompt = (1, SEQ, N_HEADS, HEAD_DIM)
    return (
        y[:SEQ].reshape(1, SEQ, D_MODEL),
        y[SEQ:].reshape(DEC_BATCH, DEC_SEQ, D_MODEL),
        k_rows[:SEQ].reshape(prompt),
        r["v_prompt"].reshape(prompt),
        conv[:2].reshape(1, 2, D_ATT),
        join_cache(k_used, r["k_rest_out"], k_rows[SEQ:].reshape(DEC_BATCH, DEC_SEQ, D_ATT)),
        join_cache(v_used, r["v_rest_out"], r["v_sample"].reshape(DEC_BATCH, DEC_SEQ, D_ATT)),
        conv[2:].reshape(DEC_BATCH, 2, D_ATT),
    )
```
